# Optimizing a Trainium2 kernel written in Bass

```python
import jax, jax.numpy as jnp
from jax import lax
import numpy as np

D_MODEL = 2048
BATCH = 1
SEQ = 256
DEPTH = 2

MEM_LEN = 256
HEAD_DIM = 128
N_MIX_HEADS = 12
N_MEM_HEADS = 4
MIX_WIDTH = N_MIX_HEADS * HEAD_DIM
MEM_WIDTH = N_MEM_HEADS * HEAD_DIM
CAT_WIDTH = MIX_WIDTH + MEM_WIDTH

Q_LORA = 512
KV_LORA = 512
QK_NOPE = 128
QK_ROPE = 64
V_HEAD = HEAD_DIM
ROPE_THETA = 10000.0
Q_BLOCK = 128
MLA_MIX_IN = Q_LORA + KV_LORA + QK_ROPE
MLA_IN = MLA_MIX_IN + MEM_WIDTH

CONV_WIDTH = 4
CHUNK = 64
GDN_MIX_IN = 4 * MIX_WIDTH + 2 * N_MIX_HEADS
GDN_IN = GDN_MIX_IN + MEM_WIDTH

D_FF = 4 * D_MODEL
ALPHA = (2 * DEPTH) ** 0.25
BETA_INIT = (8 * DEPTH) ** -0.25
N_MLA = (DEPTH + 1) // 2
N_GDN = DEPTH // 2
LN_EPS = 1e-5
RMS_EPS = 1e-6

kernel_name = "hybrid_mla_gdn_deepnorm_memory"

def layer_norm(x, g, b):
    xf = x.astype(jnp.float32)
    mu = jnp.mean(xf, -1, keepdims=True)
    var = jnp.mean(jnp.square(xf - mu), -1, keepdims=True)
    return ((xf - mu) * lax.rsqrt(var + LN_EPS) * g + b).astype(x.dtype)

def rms_norm(x, g):
    xf = x.astype(jnp.float32)
    return (xf * lax.rsqrt(jnp.mean(xf * xf, -1, keepdims=True) + RMS_EPS) * g).astype(x.dtype)

def l2_normalize(x):
    return x * lax.rsqrt(jnp.sum(x * x, -1, keepdims=True) + 1e-6)

def rope(x, cos, sin):
    half = x.shape[-1] // 2
    x1, x2 = x[..., :half], x[..., half:]
    return jnp.concatenate([x1 * cos - x2 * sin, x2 * cos + x1 * sin], -1)

def causal_block_attention(q, k, v):
    B_, S_, H, Dq = q.shape
    nb = S_ // Q_BLOCK
    qb = jnp.moveaxis(q.reshape(B_, nb, Q_BLOCK, H, Dq), 1, 0)
    kpos = jnp.arange(S_)
    scale = Dq ** -0.5

    def one_block(args):
        qi, bi = args
        s = jnp.einsum('bqhd,bkhd->bhqk', qi, k).astype(jnp.float32) * scale
        qpos = bi * Q_BLOCK + jnp.arange(Q_BLOCK)
        s = jnp.where(kpos[None, :] <= qpos[:, None], s, -jnp.inf)
        p = jax.nn.softmax(s, axis=-1).astype(v.dtype)
        return jnp.einsum('bhqk,bkhd->bqhd', p, v)

    o = lax.map(one_block, (qb, jnp.arange(nb)))
    return jnp.moveaxis(o, 0, 1).reshape(B_, S_, H, v.shape[-1])

def memory_attention(q, mem_kv):
    B_, M_, _ = mem_kv.shape
    k = mem_kv[..., :MEM_WIDTH].reshape(B_, M_, N_MEM_HEADS, HEAD_DIM)
    v = mem_kv[..., MEM_WIDTH:].reshape(B_, M_, N_MEM_HEADS, HEAD_DIM)
    s = jnp.einsum('bshd,bmhd->bhsm', q, k).astype(jnp.float32) * HEAD_DIM ** -0.5
    p = jax.nn.softmax(s, axis=-1).astype(v.dtype)
    o = jnp.einsum('bhsm,bmhd->bshd', p, v)
    return o.reshape(q.shape[0], q.shape[1], MEM_WIDTH)

def mla_mixer(h, cos, sin, q_norm, w_uq, kv_norm, w_ukv):
    B_, S_, _ = h.shape
    c_q = h[..., :Q_LORA]
    c_kv = h[..., Q_LORA:Q_LORA + KV_LORA]
    k_r = h[..., Q_LORA + KV_LORA:]
    q = (rms_norm(c_q, q_norm) @ w_uq).reshape(B_, S_, N_MIX_HEADS, QK_NOPE + QK_ROPE)
    q = jnp.concatenate([q[..., :QK_NOPE], rope(q[..., QK_NOPE:], cos, sin)], -1)
    kv = (rms_norm(c_kv, kv_norm) @ w_ukv).reshape(B_, S_, N_MIX_HEADS, QK_NOPE + V_HEAD)
    k_r = rope(k_r[:, :, None, :], cos, sin)
    k = jnp.concatenate([kv[..., :QK_NOPE], jnp.broadcast_to(k_r, (B_, S_, N_MIX_HEADS, QK_ROPE))], -1)
    v = kv[..., QK_NOPE:]
    return causal_block_attention(q, k, v).reshape(B_, S_, MIX_WIDTH)

def causal_depthwise_conv(x, w):
    C = x.shape[-1]
    return lax.conv_general_dilated(
        x, w[:, None, :].astype(x.dtype), window_strides=(1,),
        padding=[(CONV_WIDTH - 1, 0)], dimension_numbers=('NWC', 'WIO', 'NWC'),
        feature_group_count=C)

def gated_delta_chunked(q, k, v, g, beta):
    B_, S_, H, Dk = q.shape
    Dv = v.shape[-1]
    N = S_ // CHUNK

    def to_chunks(t):
        return jnp.moveaxis(t.reshape((B_, N, CHUNK) + t.shape[2:]), 2, 3)

    q = to_chunks(q * Dk ** -0.5)
    k = to_chunks(k)
    v = to_chunks(v)
    beta = to_chunks(beta)
    gc = jnp.cumsum(to_chunks(g), axis=-1)

    tril = jnp.tril(jnp.ones((CHUNK, CHUNK), bool))
    strict = jnp.tril(jnp.ones((CHUNK, CHUNK), bool), k=-1)
    diff = gc[..., :, None] - gc[..., None, :]
    decay = jnp.where(tril, jnp.exp(jnp.where(tril, diff, 0.0)), 0.0)

    kb = k * beta[..., None]
    L = jnp.where(strict, jnp.einsum('bnhcd,bnhed->bnhce', kb, k) * decay, 0.0)
    a = L + jnp.eye(CHUNK, dtype=jnp.float32)
    rhs = jnp.concatenate([v * beta[..., None], kb * jnp.exp(gc)[..., None]], -1)
    sol = lax.linalg.triangular_solve(a, rhs, left_side=True, lower=True, unit_diagonal=True)
    u, w = sol[..., :Dv], sol[..., Dv:]

    a_qk = jnp.where(tril, jnp.einsum('bnhcd,bnhed->bnhce', q, k) * decay, 0.0)
    q_dec = q * jnp.exp(gc)[..., None]
    k_dec = k * jnp.exp(gc[..., -1:] - gc)[..., None]
    g_last = jnp.exp(gc[..., -1])

    def step(state, inp):
        qd, kd, uu, ww, aqk, gl = inp
        v_new = uu - jnp.einsum('bhcd,bhde->bhce', ww, state)
        o = jnp.einsum('bhcd,bhde->bhce', qd, state) + jnp.einsum('bhce,bhef->bhcf', aqk, v_new)
        state = state * gl[..., None, None] + jnp.einsum('bhcd,bhce->bhde', kd, v_new)
        return state, o

    xs = tuple(jnp.moveaxis(t, 1, 0) for t in (q_dec, k_dec, u, w, a_qk, g_last))
    state0 = jnp.zeros((B_, H, Dk, Dv), jnp.float32)
    _, o = lax.scan(step, state0, xs)
    return jnp.transpose(o, (1, 0, 3, 2, 4)).reshape(B_, S_, H, Dv)

def gdn_mixer(h, conv_w, a_log, dt_bias, o_norm):
    B_, S_, _ = h.shape
    qkv = jax.nn.silu(causal_depthwise_conv(h[..., :3 * MIX_WIDTH], conv_w)).astype(jnp.float32)
    z = h[..., 3 * MIX_WIDTH:4 * MIX_WIDTH].astype(jnp.float32)
    a_in = h[..., 4 * MIX_WIDTH:4 * MIX_WIDTH + N_MIX_HEADS].astype(jnp.float32)
    b_in = h[..., 4 * MIX_WIDTH + N_MIX_HEADS:].astype(jnp.float32)
    shp = (B_, S_, N_MIX_HEADS, HEAD_DIM)
    q = l2_normalize(qkv[..., :MIX_WIDTH].reshape(shp))
    k = l2_normalize(qkv[..., MIX_WIDTH:2 * MIX_WIDTH].reshape(shp))
    v = qkv[..., 2 * MIX_WIDTH:].reshape(shp)
    g = -jnp.exp(a_log.astype(jnp.float32)) * jax.nn.softplus(a_in + dt_bias.astype(jnp.float32))
    beta = jax.nn.sigmoid(b_in)
    o = gated_delta_chunked(q, k, v, g, beta)
    o = rms_norm(o, o_norm.astype(jnp.float32)) * jax.nn.silu(z.reshape(shp))
    return o.reshape(B_, S_, MIX_WIDTH).astype(h.dtype)

def setup_inputs(seed: int = 0) -> dict:
    key = jax.random.key(seed)
    ks = jax.random.split(key, 24)
    f32 = jnp.float32
    nrm = lambda k, shape, scale: jax.random.normal(k, shape, f32) * scale
    gain = lambda k, shape: 1.0 + 0.02 * jax.random.normal(k, shape, f32)
    offset = jax.random.randint(ks[2], (BATCH, 1), 0, 1024, dtype=jnp.int32)
    positions = (offset + jnp.arange(SEQ, dtype=jnp.int32)[None, :]).astype(jnp.int32)
    dt = jnp.exp(jax.random.uniform(ks[11], (N_GDN, N_MIX_HEADS), f32, np.log(1e-3), np.log(1e-1)))
    return {
        "x": jax.random.normal(ks[0], (BATCH, SEQ, D_MODEL), f32),
        "mem": jax.random.normal(ks[1], (BATCH, MEM_LEN, D_MODEL), f32),
        "positions": positions,
        "mla_w_in": nrm(ks[3], (N_MLA, D_MODEL, MLA_IN), D_MODEL ** -0.5),
        "mla_q_norm": gain(ks[4], (N_MLA, Q_LORA)),
        "mla_w_uq": nrm(ks[5], (N_MLA, Q_LORA, N_MIX_HEADS * (QK_NOPE + QK_ROPE)), Q_LORA ** -0.5),
        "mla_kv_norm": gain(ks[6], (N_MLA, KV_LORA)),
        "mla_w_ukv": nrm(ks[7], (N_MLA, KV_LORA, N_MIX_HEADS * (QK_NOPE + V_HEAD)), KV_LORA ** -0.5),
        "gdn_w_in": nrm(ks[8], (N_GDN, D_MODEL, GDN_IN), D_MODEL ** -0.5),
        "gdn_conv": nrm(ks[9], (N_GDN, CONV_WIDTH, 3 * MIX_WIDTH), CONV_WIDTH ** -0.5),
        "gdn_a_log": jnp.log(jax.random.uniform(ks[10], (N_GDN, N_MIX_HEADS), f32, 1.0, 16.0)),
        "gdn_dt_bias": dt + jnp.log(-jnp.expm1(-dt)),
        "gdn_o_norm": gain(ks[12], (N_GDN, HEAD_DIM)),
        "mem_w_kv": nrm(ks[13], (DEPTH, D_MODEL, 2 * MEM_WIDTH), D_MODEL ** -0.5),
        "w_out": nrm(ks[14], (DEPTH, CAT_WIDTH, D_MODEL), CAT_WIDTH ** -0.5 * BETA_INIT),
        "ln1_g": gain(ks[15], (DEPTH, D_MODEL)),
        "ln1_b": nrm(ks[16], (DEPTH, D_MODEL), 0.02),
        "mlp_w1": nrm(ks[17], (DEPTH, D_MODEL, D_FF), D_MODEL ** -0.5),
        "mlp_w2": nrm(ks[18], (DEPTH, D_FF, D_MODEL), D_FF ** -0.5 * BETA_INIT),
        "ln2_g": gain(ks[19], (DEPTH, D_MODEL)),
        "ln2_b": nrm(ks[20], (DEPTH, D_MODEL), 0.02),
    }

def reference(x, mem, positions, mla_w_in, mla_q_norm, mla_w_uq, mla_kv_norm, mla_w_ukv,
              gdn_w_in, gdn_conv, gdn_a_log, gdn_dt_bias, gdn_o_norm, mem_w_kv, w_out,
              ln1_g, ln1_b, mlp_w1, mlp_w2, ln2_g, ln2_b):
    B_, S_, _ = x.shape
    inv_freq = 1.0 / (ROPE_THETA ** (jnp.arange(0, QK_ROPE, 2, dtype=jnp.float32) / QK_ROPE))
    ang = positions.astype(jnp.float32)[:, :, None, None] * inv_freq
    cos = jnp.cos(ang).astype(x.dtype)
    sin = jnp.sin(ang).astype(x.dtype)
    for i in range(DEPTH):
        j = i // 2
        mem_kv = mem @ mem_w_kv[i]
        if i % 2 == 0:
            h = x @ mla_w_in[j]
            mix = mla_mixer(h[..., :MLA_MIX_IN], cos, sin, mla_q_norm[j], mla_w_uq[j],
                            mla_kv_norm[j], mla_w_ukv[j])
        else:
            h = x @ gdn_w_in[j]
            mix = gdn_mixer(h[..., :GDN_MIX_IN], gdn_conv[j], gdn_a_log[j], gdn_dt_bias[j], gdn_o_norm[j])
        q_mem = h[..., -MEM_WIDTH:].reshape(B_, S_, N_MEM_HEADS, HEAD_DIM)
        mem_o = memory_attention(q_mem, mem_kv)
        y = jnp.concatenate([mix, mem_o], -1) @ w_out[i]
        x = layer_norm(ALPHA * x + y, ln1_g[i], ln1_b[i])
        ff = jnp.square(jax.nn.relu(x @ mlp_w1[i])) @ mlp_w2[i]
        x = layer_norm(ALPHA * x + ff, ln2_g[i], ln2_b[i])
    return x


_drawn_inputs = setup_inputs


def setup_inputs(seed=0):
    import zlib

    import numpy as np

    out = dict(_drawn_inputs(seed))
    spreads = {}
    factors = {'mla_q_norm': 8.0,
     'mla_kv_norm': 8.0,
     'gdn_o_norm': 29.021,
     'mem': 3.629,
     'mem_w_kv': 3.543}
    for name, (base, spread) in spreads.items():
        noise = np.random.default_rng([zlib.crc32(name.encode()), seed]).standard_normal(out[name].shape)
        drawn = base * np.exp(spread * noise) if base else spread * noise
        out[name] = __import__('jax').numpy.asarray(drawn.astype(out[name].dtype))
    for name, factor in factors.items():
        out[name] = (out[name] * factor).astype(out[name].dtype)
    return out
```

```python
from contextlib import ExitStack

import numpy as np

import concourse.bass as bass
from concourse import mybir

F32 = mybir.dt.float32
F32R = mybir.dt.float32r
BF16 = mybir.dt.bfloat16
I32 = mybir.dt.int32
ACT = mybir.ActivationFunctionType
ALU = mybir.AluOpType
AX = mybir.AxisListType

P = 128
D = 2048
S = 256
TT = S // P
KT = D // P
NH = 12
NM = 4
MIXW = NH * P
LORA = 512
ROPE = 64
HR = ROPE // 2
QKD = P + ROPE
FF = 4 * D
DEPTH = 2
ALPHA = (2 * DEPTH) ** 0.25
LN_EPS = 1e-5
RMS_EPS = 1e-6
ROPE_THETA = 10000.0
NEG = -1e30

LAST = 1
NRAW = 4
NSPLIT = 4
CK = 2
CN = 512
PANEL = KT // CK
GROUPS = FF // D
UP = D // CN
GCH = 2 * UP * PANEL

GH = 4
HG = NH // GH
CHUNK = 64
NC = S // CHUNK
TAPS = 4
CB = 3 * NH
LEVELS = 6
GDN_Z = 3 * MIXW
GDN_AB = 4 * MIXW
GDN_QM = 4 * MIXW + 2 * NH

STAGES = [
    ("memk0", 1, PANEL), ("memv0", 1, PANEL), ("cq", 1, PANEL), ("ckv", 1, PANEL), ("kr", 1, 1),
    ("qm0", 1, PANEL), ("qrope", 2, 2), ("qnope", 3, 2), ("knope", 3, 2), ("v", 3, 2),
    ("out0", UP, PANEL), ("mlp0", 2 * UP * GROUPS, PANEL),
    ("memk1", 1, PANEL), ("memv1", 1, PANEL), ("ab", 1, 1),
    *[(f"{n}{g}", 1, PANEL) for g in range(HG) for n in "qkvz"],
    ("qm1", 1, PANEL), ("out1", UP, PANEL), ("mlp1", 2 * UP * GROUPS, PANEL),
]
TURNS = [("mem0", 8), ("x", 8), ("cq", 2), ("ckv", 2), ("ln1_0", 8), ("mem1", 8), ("ln2_0", 8),
         *[(f"gdn{g}", 2) for g in range(HG)], ("ln1_1", 8)]


def positions(stages):
    at, n = {}, 0
    for name, k in stages:
        at[name] = n
        n += k
    return at, n


PANEL_AT, PANELS = positions([(n, p) for n, p, _ in STAGES])
CHUNK_AT, CHUNKS = positions([(n, p * c) for n, p, c in STAGES])
TURN_AT, NTURNS = positions(TURNS)


def chunk_uses(slot, c):
    return (c - slot) // NRAW + 1


class Buffers:
    pass


def place(nc):
    b = Buffers()
    base = 16640
    end = 229344

    def at(name, shape, dt, offset):
        size = int(np.prod(shape[1:])) * (2 if dt == BF16 else 4)
        assert offset + size <= end, name
        buffer = nc.alloc_sbuf_tensor_at(name, shape, dt, offset=offset)
        return buffer, offset + (size + 31) // 32 * 32

    b.raw, o = at("raw", [P, NRAW, CK, CN], F32, base)
    b.whi, o = at("whi", [P, NSPLIT, CK, CN], F32R, o)
    b.wlo, o = at("wlo", [P, NSPLIT, CK, CN], F32R, o)
    x_region = o
    b.xh, o = at("xh", [P, KT, S], F32R, o)
    b.xl, o = at("xl", [P, KT, S], F32R, o)
    h_region = o
    b.hh, o = at("hh", [P, KT, S], F32R, o)
    b.hl, o = at("hl", [P, KT, S], F32R, o)
    b.z, o = at("z", [P, TT, D], F32, o)
    b.ident, o = at("ident", [P, P], F32, o)
    b.identb, o = at("identb", [P, P], BF16, o)
    b.causal, o = at("causal", [P, TT, S], BF16, o)
    b.vrow, o = at("vrow", [P, 3, P], F32, o)
    b.vcol, o = at("vcol", [P, 3, P], F32, o)
    b.stats, o = at("stats", [P, TT, 4, 6], F32, o)
    b.mv, o = at("mv", [P, TT, 2], F32, o)
    b.rs, o = at("rs", [P, TT], F32, o)
    b.nmr, o = at("nmr", [P, TT], F32, o)
    b.mhalf, o = at("mhalf", [P, 16], F32, o)
    b.mx, o = at("mx", [P, 2, TT], F32, o)
    b.sums, o = at("sums", [P, 2, TT], F32, o)
    b.rinv, o = at("rinv", [P, 2, TT], F32, o)
    b.xf, o = at("xf", [P, 2, 2 * S], F32, o)
    b.km, o = at("km", [P, NM, S], F32, o)
    b.vm, o = at("vm", [P, TT, NM * P], F32, o)
    b.qm, o = at("qm", [P, NM, S], F32, o)
    stage = o
    b.tri, o = at("tri", [P, P], F32, o)
    b.blk, o = at("blk", [P, P], F32, o)
    b.ones, o = at("ones", [P, P], F32, o)
    b.negtri, o = at("negtri", [P, P], BF16, o)
    b.level, o = at("level", [P, LEVELS, P], F32, o)
    b.glog, o = at("glog", [P, TT, NH], F32, o)
    b.beta, o = at("beta", [P, TT, NH], F32, o)
    b.gcum, o = at("gcum", [P, TT, NH], F32, o)
    b.eg, o = at("eg", [P, TT, NH], F32, o)
    b.ek, o = at("ek", [P, TT, NH], F32, o)
    b.el, o = at("el", [P, NC, NH], F32, o)
    b.gt, o = at("gt", [P, 2, TT, NH], F32, o)
    b.arow, o = at("arow", [P, TT, 2 * NH], F32, o)
    b.alog, o = at("alog", [P, NH], F32, o)
    b.dtb, o = at("dtb", [P, NH], F32, o)
    b.ss, o = at("ss", [P, 3, TT * GH], F32, o)
    stage = o
    quad = [P, TT, GH, P]
    b.qr, o = at("qr", quad, F32, stage)
    b.kr, o = at("kr", quad, F32, o)
    b.vr, o = at("vr", quad, F32, o)
    b.zr, o = at("zr", quad, F32, o)
    b.kb, o = at("kb", quad, F32, o)
    b.kt, o = at("kt", quad, F32, o)
    b.kbt, o = at("kbt", quad, F32, o)
    b.qt, o = at("qt", quad, F32, o)
    b.qdt, o = at("qdt", quad, F32, o)
    b.dt, o = at("dt", quad, F32, o)
    b.nt, o = at("nt", quad, F32, o)
    b.st, o = at("st", [P, 3, GH, P], F32, o)
    b.bm = b.vn = b.qr
    b.xi = b.wt = b.kt
    b.xt = b.kbt
    b.ys = b.uu = b.qt
    b.orow = b.kb
    b.tg = b.nt
    b.aq = b.dt
    b.cv, r = at("cv", [P, GH, S], F32, h_region + 12 * S * 4)
    b.th, r = at("th", [P, GH, S], F32, h_region + KT * S * 4 + 12 * S * 4)
    b.ch, o = at("ch", [P, 8, S], F32R, stage)
    b.cl, o = at("cl", [P, 8, S], F32R, o)
    b.qn, o = at("qn", [P, NH, S], F32, o)
    b.kn, o = at("kn", [P, NH, S], F32, o)
    b.krt, o = at("krt", [P, S], F32, o)
    b.invf, o = at("invf", [P, HR], F32, o)
    b.pos, o = at("pos", [P, TT], I32, o)
    b.posf, o = at("posf", [P, TT], F32, o)
    b.ang, o = at("ang", [P, TT, HR], F32, o)
    b.turns, o = at("turns", [P, 2, TT, HR], F32, o)
    b.arg, o = at("arg", [P, 2, TT, HR], F32, o)
    b.trig, o = at("trig", [P, 2, TT, HR], F32, o)
    b.cqrow, r = at("cqrow", [P, TT, LORA], F32, h_region)
    b.ckvrow, r = at("ckvrow", [P, TT, LORA], F32, r)
    b.csq, r = at("csq", [P, TT, LORA], F32, r)
    b.css, r = at("css", [P, 2, TT], F32, r)
    b.crs, r = at("crs", [P, 2, TT], F32, r)
    b.krow, r = at("krow", [P, TT, ROPE], F32, r)
    b.krot, r = at("krot", [P, TT, 2, ROPE], F32, r)
    b.rtmp, r = at("rtmp", [P, 4, NH // 2 * HR * 2], F32, r)
    b.vrows, r = at("vrows", [P, TT, MIXW], F32, x_region)
    b.qrrow, r = at("qrrow", [P, TT, NH, ROPE], F32, r)
    b.qrt, r = at("qrt", [P, NH // 2, S], F32, r)
    b.prob, r = at("prob", [P, 2, TT, S], F32, r)
    b.probt, r = at("probt", [P, 2, 2 * S], F32, r)
    assert r <= h_region
    b.relu, o = at("relu", [P, 2, UP * S], F32, stage)
    b.mrow, o = at("mrow", [P, TT, D], F32, o)
    b.gb, o = at("gb", [P, 2, D], F32, o)
    return b


class Semaphores:

    def __init__(self, signal):
        self.raw_ready0 = signal("raw_ready0")
        self.raw_ready1 = signal("raw_ready1")
        self.raw_ready2 = signal("raw_ready2")
        self.raw_ready3 = signal("raw_ready3")
        self.hi_ready = signal("hi_ready")
        self.lo_ready = signal("lo_ready")
        self.chunk_used = signal("chunk_used")
        self.panel_free = signal("panel_free")
        self.x_in = signal("x_in")
        self.mem_half = signal("mem_half")
        self.mem_in = signal("mem_in")
        self.vec_in = signal("vec_in")
        self.pos_in = signal("pos_in")
        self.gb_in = signal("gb_in")
        self.out_done = signal("out_done")
        self.const_set = signal("const_set")
        self.vec_t = signal("vec_t")
        self.vcol_set = signal("vcol_set")
        self.trig_out = signal("trig_out")
        self.turned = signal("turned")
        self.turn_f = signal("turn_f")
        self.turn_hi = signal("turn_hi")
        self.turn_lo = signal("turn_lo")
        self.z_ready = signal("z_ready")
        self.z_sum = signal("z_sum")
        self.pool_step = signal("pool_step")
        self.dve_step = signal("dve_step")
        self.act_step = signal("act_step")
        self.stats_in = signal("stats_in")
        self.ln_mv = signal("ln_mv")
        self.ln_rs = signal("ln_rs")
        self.ln_n = signal("ln_n")
        self.sq_done = signal("sq_done")
        self.hid_hi = signal("hid_hi")
        self.hid_lo = signal("hid_lo")
        self.fin = signal("fin")
        self.c_sum = signal("c_sum")
        self.c_rs = signal("c_rs")
        self.c_norm = signal("c_norm")
        self.kr_rows = signal("kr_rows")
        self.trig_set = signal("trig_set")
        self.rot_done = signal("rot_done")
        self.rot_t = signal("rot_t")
        self.rot_out = signal("rot_out")
        self.q_rows = signal("q_rows")
        self.masks_set = signal("masks_set")
        self.gate_in = signal("gate_in")
        self.ab_rows = signal("ab_rows")
        self.g_raw = signal("g_raw")
        self.e_raw = signal("e_raw")
        self.l_raw = signal("l_raw")
        self.gates_set = signal("gates_set")
        self.p_gc = signal("p_gc")
        self.p_gl = signal("p_gl")
        self.gcum_set = signal("gcum_set")
        self.eg_set = signal("eg_set")
        self.conv0 = signal("conv0")
        self.conv1 = signal("conv1")
        self.tanh1 = signal("tanh1")
        self.cv_set = signal("cv_set")
        self.cv_t = signal("cv_t")
        self.rows_set = signal("rows_set")
        self.z_half = signal("z_half")
        self.z_tanh = signal("z_tanh")
        self.z_set = signal("z_set")
        self.g_ss = signal("g_ss")
        self.g_rs = signal("g_rs")
        self.kn_set = signal("kn_set")
        self.kb_set = signal("kb_set")
        self.qd_set = signal("qd_set")
        self.kd_set = signal("kd_set")
        self.tg_set = signal("tg_set")
        self.p_kt = signal("p_kt")
        self.a_kt = signal("a_kt")
        self.p_kbt = signal("p_kbt")
        self.a_kbt = signal("a_kbt")
        self.p_qt = signal("p_qt")
        self.a_qt = signal("a_qt")
        self.p_qdt = signal("p_qdt")
        self.a_qdt = signal("a_qdt")
        self.p_gb = signal("p_gb")
        self.d_diff = signal("d_diff")
        self.a_dec = signal("a_dec")
        self.p_l = signal("p_l")
        self.d_nt = signal("d_nt")
        self.p_aq = signal("p_aq")
        self.d_aq = signal("d_aq")
        self.bm_set = signal("bm_set")
        self.p_y = signal("p_y")
        self.a_y = signal("a_y")
        self.d_x = signal("d_x")
        self.d_xt = signal("d_xt")
        self.p_z = signal("p_z")
        self.p_zt = signal("p_zt")
        self.p_w = signal("p_w")
        self.a_w = signal("a_w")
        self.p_u = signal("p_u")
        self.d_u = signal("d_u")
        self.p_vn = signal("p_vn")
        self.d_vn = signal("d_vn")
        self.p_ds = signal("p_ds")
        self.d_s = signal("d_s")
        self.pool_s = signal("pool_s")
        self.p_o = signal("p_o")
        self.a_o = signal("a_o")
        self.o_ss = signal("o_ss")
        self.o_rs = signal("o_rs")
        self.or_set = signal("or_set")
        self.scored = signal("scored")
        self.bias_set = signal("bias_set")
        self.exp_done = signal("exp_done")
        self.norm_done = signal("norm_done")
        self.pt_done = signal("pt_done")
        self.pt_out = signal("pt_out")
        self.o_done = signal("o_done")
        self.o_hi = signal("o_hi")
        self.o_lo = signal("o_lo")
        self.raw_ready = [self.raw_ready0, self.raw_ready1, self.raw_ready2, self.raw_ready3]



def build(nc, x, mem, positions_, mla_w_in, mla_q_norm, mla_w_uq, mla_kv_norm, mla_w_ukv, gdn_w_in, gdn_conv,
          gdn_a_log, gdn_dt_bias, gdn_o_norm, mem_w_kv, w_out, ln1_g, ln1_b, mlp_w1, mlp_w2, ln2_g, ln2_b, out):
    with ExitStack() as ctx:
        b = place(nc)
        sem = Semaphores(lambda name: ctx.enter_context(nc.semaphore(name)))
        panel_ps = [ctx.enter_context(nc.psum_tensor(f"panel{i}", [P, 2, 512], F32)) for i in range(2)]
        turn_ps = [ctx.enter_context(nc.psum_tensor(f"turn{i}", [P, 512], F32)) for i in range(2)]
        pt_ps = ctx.enter_context(nc.psum_tensor("pt", [P, 512], F32))
        o_ps = ctx.enter_context(nc.psum_tensor("o", [P, 512], F32))
        block = ctx.enter_context(nc.Block())
        scale_mla = float(QKD) ** -0.5
        scale_mem = float(P) ** -0.5
        ctx.enter_context(nc.allow_non_contiguous_dma(reason="short rows of small tensors"))

        def norm_cols(which, l):
            return {"g1": 0, "b1": 32, "g2": 64, "b2": 96}[which] + 16 * l

        def vcol(tile, c):
            return b.vcol[:, tile, c:c + 1]

        @block.sync
        def _(sp):
            def load(c, src, off=0):
                slot = c % NRAW
                if c >= NRAW:
                    sp.wait_ge(sem.lo_ready, off + (c - NRAW + 1))
                inc = 32 // len(src)
                for dst, s in src:
                    sp.dma_start(dst(slot), s).then_inc(sem.raw_ready[slot], inc)

            def whole(w, kt, cols):
                return [(lambda slot: b.raw[:, slot],
                         w[kt * P:(kt + CK) * P, cols].rearrange("(t p) n -> p t n", p=P))]

            def panel(c0, w, n0, chunks=PANEL):
                for ci in range(chunks):
                    load(c0 + ci, whole(w, ci * CK, slice(n0, n0 + CN)))

            def heads_of(w, kt, width, h0, nh, lo, hi):
                out_ = []
                for k in range(CK):
                    src = w[(kt + k) * P:(kt + k + 1) * P, :].rearrange("p (h c) -> p h c", c=width)[:, h0:h0 + nh, lo:hi]
                    n = nh * (hi - lo)
                    out_.append((lambda slot, k=k, n=n, c=hi - lo:
                                 b.raw[:, slot, k, 0:n].rearrange("p (h c) -> p h c", c=c), src))
                return out_

            def gain_rows(g, o):
                sp.dma_start(b.gb[:, 0, :], g.to_broadcast((P, D))).then_inc(sem.gb_in, 16)
                sp.dma_start(b.gb[:, 1, :], o.to_broadcast((P, D))).then_inc(sem.gb_in, 16)

            def mlp(l, name):
                c0 = CHUNK_AT[name]
                with sp.Fori(0, GROUPS) as g:
                    for u in range(UP):
                        for ci in range(PANEL):
                            load(c0 + u * PANEL + ci,
                                 [(lambda slot: b.raw[:, slot],
                                   mlp_w1[l, ci * CK * P:(ci + 1) * CK * P, bass.ds(g * D + u * CN, CN)]
                                   .rearrange("(t p) n -> p t n", p=P))], g * GCH)
                    for u in range(UP):
                        for ci in range(PANEL):
                            load(c0 + (UP + u) * PANEL + ci,
                                 [(lambda slot: b.raw[:, slot],
                                   mlp_w2[l, bass.ds(g * D + ci * CK * P, CK * P), u * CN:(u + 1) * CN]
                                   .rearrange("(t p) n -> p t n", p=P))], g * GCH)

            panel(CHUNK_AT["memk0"], mem_w_kv[0], 0)
            panel(CHUNK_AT["memv0"], mem_w_kv[0], CN)
            panel(CHUNK_AT["cq"], mla_w_in[0], 0)
            panel(CHUNK_AT["ckv"], mla_w_in[0], LORA)
            load(CHUNK_AT["kr"], [(lambda slot: b.raw[:, slot].rearrange("p t (k c) -> p (t k) c", c=ROPE),
                                   mla_w_in[0, :, 2 * LORA:2 * LORA + ROPE].rearrange("(t p) n -> p t n", p=P))])
            panel(CHUNK_AT["qm0"], mla_w_in[0], 2 * LORA + ROPE)
            for name, w, width, nh, lo, hi in (("qrope", mla_w_uq, QKD, 6, P, QKD), ("qnope", mla_w_uq, QKD, 4, 0, P),
                                               ("knope", mla_w_ukv, 2 * P, 4, 0, P), ("v", mla_w_ukv, 2 * P, 4, P, 2 * P)):
                for i in range(NH // nh):
                    for ci in range(2):
                        load(CHUNK_AT[name] + 2 * i + ci, heads_of(w[0], ci * CK, width, i * nh, nh, lo, hi))
            for u in range(UP):
                if u == 2:
                    sp.wait_ge(sem.o_lo, NH + NM)
                    gain_rows(ln1_g[0:1, :], ln1_b[0:1, :])
                    sp.dma_start(b.mrow[:, :, :], mem[0].rearrange("(t p) n -> p t n", p=P)).then_inc(sem.mem_in, 16)
                panel(CHUNK_AT["out0"] + u * PANEL, w_out[0], u * CN)
            mlp(0, "mlp0")
            sp.wait_ge(sem.z_ready, 2)
            gain_rows(ln2_g[0:1, :], ln2_b[0:1, :])
            panel(CHUNK_AT["memk1"], mem_w_kv[1], 0)
            panel(CHUNK_AT["memv1"], mem_w_kv[1], CN)
            load(CHUNK_AT["ab"], [(lambda slot: b.raw[:, slot].rearrange("p t (k c) -> p (t k) c", c=ROPE),
                                   gdn_w_in[0, :, GDN_AB:GDN_AB + ROPE].rearrange("(t p) n -> p t n", p=P))])
            for g in range(HG):
                for i, n in enumerate("qkvz"):
                    panel(CHUNK_AT[f"{n}{g}"], gdn_w_in[0], i * MIXW + g * CN)
            panel(CHUNK_AT["qm1"], gdn_w_in[0], GDN_QM)
            for u in range(UP):
                if u == 2:
                    sp.wait_ge(sem.o_lo, NH + 2 * NM)
                    gain_rows(ln1_g[1:2, :], ln1_b[1:2, :])
                panel(CHUNK_AT["out1"] + u * PANEL, w_out[1], u * CN)
            mlp(1, "mlp1")
            sp.wait_ge(sem.z_ready, 4)
            gain_rows(ln2_g[1:2, :], ln2_b[1:2, :])
            for j in range(4):
                for t in range(TT):
                    sp.wait_ge(sem.fin, 2 * j + t + 1)
                    c = slice(j * CN, (j + 1) * CN)
                    sp.dma_start(out[0, t * P:(t + 1) * P, c], b.z[:, t, c]).then_inc(sem.out_done, 16)
            sp.wait_ge(sem.out_done, 16 * 8)

        @block.tensor
        def _(pe):
            def panel_t(p, c0, chunks, ah, al, ready, off=0, poff=0, part=None):
                ps = panel_ps[p % 2]
                first, after = part or (0, chunks)
                if p >= 2 and first == 0:
                    pe.wait_ge(sem.panel_free, poff + (p - 1))
                for ci in range(first, after):
                    c = c0 + ci
                    slot = c % NSPLIT
                    pe.wait_ge(sem.lo_ready, off + (c + 1))
                    ready(ci)
                    for j in range(4):
                        o = ps[:, j // 2, (j % 2) * S:(j % 2 + 1) * S]
                        cols = slice(j * P, (j + 1) * P)
                        for k in range(CK):
                            kt = ci * CK + k
                            start = ci == 0 and k == 0 and j % 2 == 0
                            stop = ci == chunks - 1 and k == CK - 1
                            nc.tensor.matmul(o, b.whi[:, slot, k, cols], ah[:, kt, :], start=start, stop=False,
                                             skip_group_check=True)
                            nc.tensor.matmul(o, b.whi[:, slot, k, cols], al[:, kt, :], start=False, stop=False,
                                             skip_group_check=True)
                            last = nc.tensor.matmul(o, b.wlo[:, slot, k, cols], ah[:, kt, :], start=False,
                                                    stop=stop, skip_group_check=True)
                    last.then_inc(sem.chunk_used, 1)

            def panel_r(p, c0, chunks, ah, al, ready, n=CN, ck=CK, off=0, poff=0, part=None):
                ps = panel_ps[p % 2]
                first, after = part or (0, chunks)
                if p >= 2 and first == 0:
                    pe.wait_ge(sem.panel_free, poff + (p - 1))
                for ci in range(first, after):
                    c = c0 + ci
                    slot = c % NSPLIT
                    pe.wait_ge(sem.lo_ready, off + (c + 1))
                    ready(ci)
                    hi = b.whi[:, slot].rearrange("p t (k c) -> p (t k) c", c=CN * CK // ck)
                    lo = b.wlo[:, slot].rearrange("p t (k c) -> p (t k) c", c=CN * CK // ck)
                    for t in range(TT):
                        for k in range(ck):
                            kt = ci * ck + k
                            toks = slice(t * P, (t + 1) * P)
                            start = ci == 0 and k == 0
                            stop = ci == chunks - 1 and k == ck - 1
                            nc.tensor.matmul(ps[:, t, 0:n], ah[:, kt, toks], hi[:, k, 0:n], start=start, stop=False)
                            nc.tensor.matmul(ps[:, t, 0:n], ah[:, kt, toks], lo[:, k, 0:n], start=False, stop=False)
                            last = nc.tensor.matmul(ps[:, t, 0:n], al[:, kt, toks], hi[:, k, 0:n], start=False,
                                                    stop=stop)
                    last.then_inc(sem.chunk_used, 1)

            def turn(g, src, kts):
                if g >= 2:
                    pe.wait_ge(sem.turn_f, g - 1)
                for i in range(2):
                    for t in range(TT):
                        kt = kts + i
                        last = nc.tensor.transpose(turn_ps[g % 2][:, (i * TT + t) * P:(i * TT + t + 1) * P],
                                                   src[:, t, kt * P:(kt + 1) * P], b.ident[:, :])
                last.then_inc(sem.turned, 1)

            def after_turn(name, per=CK):
                return lambda ci: pe.wait_ge(sem.turn_lo, TURN_AT[name] + (ci + 1) * per // 2)

            pe.wait_ge(sem.const_set, 1)
            pe.wait_ge(sem.mem_half, 16)
            for k in range(8):
                if k == 4:
                    pe.wait_ge(sem.mem_in, 16)
                turn(TURN_AT["mem0"] + k, b.mrow, 2 * k)
            pe.wait_ge(sem.x_in, 16)
            for k in range(PANEL):
                panel_t(PANEL_AT["memk0"], CHUNK_AT["memk0"], PANEL, b.hh, b.hl, after_turn("mem0"), part=(k, k + 1))
                turn(TURN_AT["x"] + k, b.z, 2 * k)
            pe.wait_ge(sem.vec_in, 16 * 9)
            for i, rows in enumerate((P, 9 + CB, 3 * CB)):
                last = nc.tensor.transpose(pt_ps[:, i * P:i * P + rows], b.vrow[0:rows, i, :], b.ident[0:rows, 0:rows])
            last.then_inc(sem.vec_t, 1)
            panel_r(PANEL_AT["memv0"], CHUNK_AT["memv0"], PANEL, b.hh, b.hl, after_turn("mem0"))
            panel_r(PANEL_AT["cq"], CHUNK_AT["cq"], PANEL, b.xh, b.xl, after_turn("x"))
            panel_r(PANEL_AT["ckv"], CHUNK_AT["ckv"], PANEL, b.xh, b.xl, after_turn("x"))
            pe.wait_ge(sem.c_norm, 1)
            for k in range(2):
                turn(TURN_AT["cq"] + k, b.cqrow, 2 * k)
            panel_r(PANEL_AT["kr"], CHUNK_AT["kr"], 1, b.xh, b.xl, after_turn("x", KT), n=ROPE, ck=KT)
            panel_t(PANEL_AT["qm0"], CHUNK_AT["qm0"], PANEL, b.xh, b.xl, after_turn("x"))
            pe.wait_ge(sem.c_norm, 2)
            for k in range(2):
                turn(TURN_AT["ckv"] + k, b.ckvrow, 2 * k)
            pe.wait_ge(sem.rot_done, 1)
            pe.wait_ge(sem.vcol_set, 1)
            for t in range(TT):
                last = nc.tensor.transpose(pt_ps[:, t * P:(t + 1) * P],
                                           b.krot[:, t].rearrange("p a c -> p (a c)"), b.ident[:, :])
            last.then_inc(sem.rot_t, 1)
            for i in range(2):
                panel_r(PANEL_AT["qrope"] + i, CHUNK_AT["qrope"] + 2 * i, 2, b.ch, b.cl, after_turn("cq"), n=6 * ROPE)
            for i in range(3):
                panel_t(PANEL_AT["qnope"] + i, CHUNK_AT["qnope"] + 2 * i, 2, b.ch, b.cl, after_turn("cq"))
            for i in range(3):
                panel_t(PANEL_AT["knope"] + i, CHUNK_AT["knope"] + 2 * i, 2, b.ch[:, 4:8, :], b.cl[:, 4:8, :],
                        after_turn("ckv"))
            for i in range(3):
                panel_r(PANEL_AT["v"] + i, CHUNK_AT["v"] + 2 * i, 2, b.ch[:, 4:8, :], b.cl[:, 4:8, :],
                        after_turn("ckv"))
            pe.wait_ge(sem.rot_done, 3)
            for g in range(3):
                pe.wait_ge(sem.rot_out, g + 1)
                for i in range(2):
                    for t in range(TT):
                        pair = 2 * g + i
                        last = nc.tensor.transpose(
                            pt_ps[:, (i * TT + t) * P:(i * TT + t + 1) * P],
                            b.qrrow[:, t, 2 * pair:2 * pair + 2, :].rearrange("p a c -> p (a c)"), b.ident[:, :])
                last.then_inc(sem.rot_t, 1)

            def scores(n, causal, q, k, rope):
                ps = turn_ps[n % 2]
                if n >= 2:
                    pe.wait_ge(sem.exp_done, n - 1)
                if causal:
                    nc.tensor.matmul(ps[:, :], b.identb[:, :], b.causal[:, :, :].rearrange("p t s -> p (t s)"),
                                     start=True, stop=False, skip_group_check=True)
                for t in range(TT):
                    toks = slice(t * P, (t + 1) * P)
                    nk = P * (t + 1) if causal else S
                    last = nc.tensor.matmul(ps[:, t * S:t * S + nk], q[:, toks], k[:, 0:nk], start=not causal and t == 0,
                                            stop=not rope, skip_group_check=True)
                    if rope:
                        lo, pair = rope
                        last = nc.tensor.matmul(ps[:, t * S:t * S + nk], b.qrt[lo:lo + ROPE, pair, toks],
                                                b.krt[lo:lo + ROPE, 0:nk], start=False, stop=True,
                                                skip_group_check=True)
                last.then_inc(sem.scored, 1)

            def key_blocks(n):
                return [(kb, t) for kb in range(TT) for t in range(TT) if n >= NH or t >= kb]

            def turn_probs(n):
                pe.wait_ge(sem.norm_done, n + 1)
                if n >= 1:
                    pe.wait_ge(sem.pt_out, n)
                for i, (kb, t) in enumerate(key_blocks(n)):
                    last = nc.tensor.transpose(pt_ps[:, i * P:(i + 1) * P],
                                               b.prob[:, n % 2, t, kb * P:(kb + 1) * P], b.ident[:, :])
                last.then_inc(sem.pt_done, 1)

            def values(n, v):
                pe.wait_ge(sem.pt_out, n + 1)
                if n >= 1:
                    pe.wait_ge(sem.o_lo, n)
                blocks = key_blocks(n)
                for kb in range(TT):
                    tiles = [t for k, t in blocks if k == kb]
                    i = blocks.index((kb, tiles[0])) * P
                    last = nc.tensor.matmul(o_ps[:, tiles[0] * P:S], v(kb), b.probt[:, n % 2, i:i + len(tiles) * P],
                                            start=kb == 0, stop=kb == TT - 1, skip_group_check=True)
                last.then_inc(sem.o_done, 1)

            def attention(n0, heads):
                n = len(heads)
                for i in range(n + 3):
                    if i < n:
                        scores(n0 + i, heads[i]["causal"], heads[i]["q"], heads[i]["k"], heads[i]["rope"])
                    if 2 <= i < n + 2:
                        turn_probs(n0 + i - 2)
                    if i >= 3:
                        values(n0 + i - 3, heads[i - 3]["v"])

            pe.wait_ge(sem.rot_out, 4)
            pe.wait_ge(sem.const_set, 2)
            pe.wait_ge(sem.panel_free, PANEL_AT["out0"])
            mem_heads = [dict(causal=False, q=b.qm[:, h, :], k=b.km[:, h, :], rope=None,
                              v=lambda kb, h=h: b.vm[:, kb, h * P:(h + 1) * P]) for h in range(NM)]
            attention(0, [dict(causal=True, q=b.qn[:, h, :], k=b.kn[:, h, :], rope=(ROPE * (h % 2), h // 2),
                               v=lambda kb, h=h: b.vrows[:, kb, h * P:(h + 1) * P]) for h in range(NH)] + mem_heads)

            pe.wait_ge(sem.o_lo, NH + NM)
            for u in range(UP):
                panel_r(PANEL_AT["out0"] + u, CHUNK_AT["out0"] + u * PANEL, PANEL, b.hh, b.hl, lambda ci: None)

            def norm_turns(name, k0, first, after):
                for k in range(first, after):
                    pe.wait_ge(sem.ln_n, k0 + 2 * (k // 2) + 2)
                    turn(TURN_AT[name] + k, b.z, 2 * k)

            def mlp(l, name, turned, k0):
                p0, c0 = PANEL_AT[name], CHUNK_AT[name]
                for k in range(PANEL // 2):
                    norm_turns(turned, k0, 2 * k, 2 * k + 2)
                    panel_t(p0, c0, PANEL, b.xh, b.xl, after_turn(turned), part=(k, k + 1))
                mlp_group(l, name, turned, 0, PANEL // 2)
                with pe.Fori(1, GROUPS) as g:
                    mlp_group(l, name, turned, g)

            def mlp_group(l, name, turned, g, done=0):
                p0, c0 = PANEL_AT[name], CHUNK_AT[name]
                off, poff = g * GCH, g * 2 * UP
                for u in range(UP):
                    panel_t(p0 + u, c0 + u * PANEL, PANEL, b.xh, b.xl, after_turn(turned), off, poff,
                            part=(done if u == 0 else 0, PANEL))
                for u in range(UP):
                    panel_r(p0 + UP + u, c0 + (UP + u) * PANEL, PANEL, b.hh, b.hl,
                            lambda ci: pe.wait_ge(sem.hid_lo, g * UP + (GROUPS * UP * l + ci * CK // UP + 1)),
                            off=off, poff=poff)

            mlp(0, "mlp0", "ln1_0", 0)

            pe.wait_ge(sem.mem_in, 32)
            for k in range(PANEL // 2):
                for i in (2 * k, 2 * k + 1):
                    turn(TURN_AT["mem1"] + i, b.mrow, 2 * i)
                panel_t(PANEL_AT["memk1"], CHUNK_AT["memk1"], PANEL, b.hh, b.hl, after_turn("mem1"), part=(k, k + 1))
            panel_t(PANEL_AT["memk1"], CHUNK_AT["memk1"], PANEL, b.hh, b.hl, after_turn("mem1"), part=(PANEL // 2, PANEL))
            for k in range(PANEL // 2):
                panel_r(PANEL_AT["memv1"], CHUNK_AT["memv1"], PANEL, b.hh, b.hl, after_turn("mem1"), part=(k, k + 1))
                norm_turns("ln2_0", 8, 2 * k, 2 * k + 2)
            panel_r(PANEL_AT["memv1"], CHUNK_AT["memv1"], PANEL, b.hh, b.hl, after_turn("mem1"), part=(PANEL // 2, PANEL))
            panel_r(PANEL_AT["ab"], CHUNK_AT["ab"], 1, b.xh, b.xl, after_turn("ln2_0", KT), n=ROPE, ck=KT)

            side_ps = [pt_ps, o_ps]

            def conv_turns(g, i):
                p = PANEL_AT[f"q{g}"] + i
                pe.wait_ge(sem.cv_set, 3 * g + i + 1)
                for t in range(TT):
                    for h in range(GH):
                        last = nc.tensor.transpose(panel_ps[p % 2][:, t, h * P:(h + 1) * P],
                                                   b.cv[:, h, t * P:(t + 1) * P], b.ident[:, :])
                last.then_inc(sem.cv_t, 1)

            def each(f, bank, then):
                for h in range(GH):
                    last = f(h, bank[:, h * P:(h + 1) * P], h == 0)
                last.then_inc(then, 1)

            def turned_panel(name, first, after):
                panel_t(PANEL_AT[name], CHUNK_AT[name], PANEL, b.xh, b.xl, after_turn("ln2_0"), part=(first, after))

            def beside(g, i0, n=1):
                for i in range(i0, i0 + n):
                    if i < PANEL:
                        panel_r(PANEL_AT[f"z{g}"], CHUNK_AT[f"z{g}"], PANEL, b.xh, b.xl, after_turn("ln2_0"),
                                part=(i, i + 1))
                    else:
                        panel_t(PANEL_AT[f"z{g}"] + 1, CHUNK_AT[f"z{g}"] + PANEL, PANEL, b.xh, b.xl,
                                after_turn("ln2_0"), part=(i - PANEL, i - PANEL + 1))

            def gdn(g):
                n0 = g * TT
                tiles = range(TT)
                beside(g, 0, 4)
                conv_turns(g, 2)
                for t in tiles:
                    pe.wait_ge(sem.kn_set, g + 1)
                    if g:
                        pe.wait_ge(sem.turn_f, TURN_AT[f"gdn{g}"])
                    else:
                        pe.wait_ge(sem.gcum_set, 1)
                    each(lambda h, o, s_: nc.tensor.transpose(o, b.kr[:, t, h, :], b.ident[:, :]), turn_ps[t], sem.p_kt)
                for t in tiles:
                    pe.wait_ge(sem.kb_set, g + 1)
                    if g:
                        pe.wait_ge(sem.a_o, g * NC)
                    each(lambda h, o, s_: nc.tensor.transpose(o, b.kb[:, t, h, :], b.ident[:, :]), side_ps[t], sem.p_kbt)
                for t in tiles:
                    pe.wait_ge(sem.a_kt, n0 + t + 1)
                    each(lambda h, o, s_: nc.tensor.transpose(o, b.qr[:, t, h, :], b.ident[:, :]), turn_ps[t], sem.p_qt)
                for t in tiles:
                    pe.wait_ge(sem.tg_set, n0 + t + 1)
                    pe.wait_ge(sem.a_kbt, n0 + t + 1)
                    nc.tensor.matmul(side_ps[t][:, :], b.ones[:, :], b.tg[:, t].rearrange("p h c -> p (h c)"),
                                     start=True, stop=False, skip_group_check=True)
                    for h in range(GH):
                        last = nc.tensor.matmul(side_ps[t][:, h * P:(h + 1) * P], b.identb[:, :], b.negtri[:, :],
                                                start=False, stop=h == GH - 1, skip_group_check=True)
                    last.then_inc(sem.p_gb, 1)
                for t in tiles:
                    pe.wait_ge(sem.qd_set, g + 1)
                    pe.wait_ge(sem.a_qt, n0 + t + 1)
                    each(lambda h, o, s_: nc.tensor.transpose(o, b.qr[:, t, h, :], b.ident[:, :]), turn_ps[t], sem.p_qdt)
                beside(g, 4)
                for t in tiles:
                    pe.wait_ge(sem.d_diff, n0 + t + 1)
                    each(lambda h, o, s_: nc.tensor.matmul(o, b.kt[:, t, h, :], b.kbt[:, t, h, :], start=s_, stop=True,
                                                           skip_group_check=True), side_ps[t], sem.p_l)
                for t in tiles:
                    pe.wait_ge(sem.a_qdt, n0 + t + 1)
                    each(lambda h, o, s_: nc.tensor.matmul(o, b.kt[:, t, h, :], b.qt[:, t, h, :], start=s_, stop=True,
                                                           skip_group_check=True), turn_ps[t], sem.p_aq)
                beside(g, 5, 2)
                for l in range(LEVELS):
                    m0 = (g * LEVELS + l) * TT
                    for t in tiles:
                        pe.wait_ge(sem.bm_set, m0 + t + 1)
                        if l == 0:
                            pe.wait_ge(sem.d_aq, n0 + t + 1)
                            each(lambda h, o, s_: nc.tensor.transpose(o, b.bm[:, t, h, :], b.ident[:, :]),
                                 turn_ps[t], sem.p_y)
                        else:
                            pe.wait_ge(sem.d_x, (g * (LEVELS - 1) + l - 1) * TT + t + 1)
                            each(lambda h, o, s_: nc.tensor.matmul(o, b.bm[:, t, h, :], b.xi[:, t, h, :], start=s_,
                                                                   stop=True, skip_group_check=True),
                                 turn_ps[t], sem.p_y)
                    if l == 0:
                        continue
                    beside(g, 6 + l)
                    for t in tiles:
                        pe.wait_ge(sem.a_y, m0 + t + 1)
                        pe.wait_ge(sem.d_xt, m0 - TT + t + 1)
                        if l < LEVELS - 1:
                            each(lambda h, o, s_: nc.tensor.matmul(o, b.xt[:, t, h, :], b.ys[:, t, h, :], start=s_,
                                                                   stop=True, skip_group_check=True),
                                 turn_ps[t], sem.p_z)
                        each(lambda h, o, s_: nc.tensor.matmul(o, b.ys[:, t, h, :], b.xt[:, t, h, :], start=s_,
                                                               stop=True, skip_group_check=True),
                             side_ps[t], sem.p_zt)
                for t in tiles:
                    pe.wait_ge(sem.d_xt, (g + 1) * LEVELS * TT - TT + t + 1)
                    pe.wait_ge(sem.kd_set, g + 1)
                    each(lambda h, o, s_: nc.tensor.matmul(o, b.kb[:, t, h, :], b.xt[:, t, h, :], start=s_, stop=True,
                                                           skip_group_check=True), turn_ps[t], sem.p_w)
                    each(lambda h, o, s_: nc.tensor.matmul(o, b.xt[:, t, h, :], b.vr[:, t, h, :], start=s_, stop=True,
                                                           skip_group_check=True), side_ps[t], sem.p_u)
                for t in tiles:
                    pe.wait_ge(sem.a_w, n0 + t + 1)
                    pe.wait_ge(sem.d_u, n0 + t + 1)
                for j in range(NC):
                    t = j // 2
                    r = slice(CHUNK * (j % 2), CHUNK * (j % 2 + 1))
                    m = g * NC + j
                    state = b.st[:, j % 2]
                    if j:
                        pe.wait_ge(sem.d_s, g * (NC - 1) + j)
                        each(lambda h, o, s_: nc.tensor.matmul(o[r, :], b.wt[:, t, h, r], state[:, h, :], start=s_,
                                                               stop=True, skip_group_check=True), turn_ps[0], sem.p_vn)
                        for h in range(GH):
                            nc.tensor.matmul(side_ps[t][r, h * P:(h + 1) * P], b.qdt[:, t, h, r], state[:, h, :],
                                             start=h == 0, stop=False, skip_group_check=True)
                        beside(g, 6 + LEVELS - 1 + j)
                    pe.wait_ge(sem.d_vn, m + 1)
                    if j < NC - 1:
                        each(lambda h, o, s_: nc.tensor.matmul(o, b.kr[r, t, h, :], b.vn[r, 0, h, :], start=s_, stop=True,
                                                               skip_group_check=True), turn_ps[1], sem.p_ds)
                    each(lambda h, o, s_: nc.tensor.matmul(o[r, :], b.aq[r, t, h, r], b.vn[r, 0, h, :],
                                                           start=j == 0 and s_, stop=True, skip_group_check=True),
                         side_ps[t], sem.p_o)
                beside(g, 6 + LEVELS - 1 + NC)
                if g < HG - 1:
                    turned_panel(f"k{g + 1}", 0, 3)
                pe.wait_ge(sem.or_set, g + 1)
                for k in range(2):
                    turn(TURN_AT[f"gdn{g}"] + k, b.orow[:, :].rearrange("p t h c -> p t (h c)"), 2 * k)

            turned_panel("q0", 0, 2)
            pe.wait_ge(sem.gates_set, 1)
            pe.wait_ge(sem.masks_set, 1)
            pe.wait_ge(sem.turn_f, TURN_AT["gdn0"])
            glog = b.glog[:, :, :].rearrange("p t h -> p (t h)")
            nc.tensor.matmul(turn_ps[0][:, 0:TT * NH], b.tri[:, :], glog, start=True, stop=True)
            nc.tensor.matmul(turn_ps[0][:, 32:32 + TT * NH], b.blk[:, :], glog, start=False, stop=True,
                             skip_group_check=True)
            for j in range(NC):
                c = CHUNK * (j % 2)
                last = nc.tensor.matmul(turn_ps[1][:, j * NH:(j + 1) * NH], b.blk[:, c:c + 1].to_broadcast((P, P)),
                                        b.glog[:, j // 2, :], start=j == 0, stop=True, skip_group_check=True)
            last.then_inc(sem.p_gc, 1)
            turned_panel("q0", 2, PANEL)
            for g in range(HG):
                for i in (1, 2):
                    name = "qkv"[i] + str(g)
                    place = PANEL - 1 if i == 1 else PANEL // 2 + 1
                    turned_panel(name, 3 if g and i == 1 else 0, place)
                    conv_turns(g, i - 1)
                    turned_panel(name, place, PANEL)
                gdn(g)
            pe.wait_ge(sem.turn_lo, TURN_AT["ln1_1"])
            pe.wait_ge(sem.panel_free, PANEL_AT["out1"])
            attention(NH + NM, mem_heads)
            pe.wait_ge(sem.o_lo, NH + 2 * NM)
            for u in range(UP):
                panel_r(PANEL_AT["out1"] + u, CHUNK_AT["out1"] + u * PANEL, PANEL, b.hh, b.hl, lambda ci: None)
            mlp(1, "mlp1", "ln1_1", 16)

        @block.scalar
        def _(act):
            def split(c, off=0):
                slot = c % NRAW
                uses = chunk_uses(slot, c)
                act.wait_ge(sem.raw_ready[slot], off * (32 // NRAW) + 32 * uses)
                if c >= NSPLIT:
                    act.wait_ge(sem.chunk_used, off + (c - NSPLIT + 1))
                nc.scalar.activation(b.whi[:, c % NSPLIT], b.raw[:, slot], ACT.Copy).then_inc(sem.hi_ready, 1)

            fed = [0]

            def feed(k):
                for _ in range(k):
                    if fed[0] < CHUNKS:
                        split(fed[0])
                        fed[0] += 1

            def panel_end(name, i=0, off=0):
                chunks = {n: c for n, _, c in STAGES}[name]
                c = CHUNK_AT[name] + (i + 1) * chunks
                act.wait_ge(sem.chunk_used, off + c)

            def banks(name, i=0):
                return panel_ps[(PANEL_AT[name] + i) % 2]

            def split_turn(g, dst, kt):
                act.wait_ge(sem.turn_f, g + 1)
                nc.scalar.activation(dst[:, kt:kt + 2, :].rearrange("p k s -> p (k s)"), b.xf[:, g % 2, :],
                                     ACT.Copy).then_inc(sem.turn_hi, 1)

            def take_t(name, i, dst, h0, scale):
                panel_end(name, i)
                for j in range(2):
                    last = nc.scalar.activation(dst[:, h0 + 2 * j:h0 + 2 * j + 2, :].rearrange("p k s -> p (k s)"),
                                                banks(name, i)[:, j, :], ACT.Copy, scale=scale)
                last.then_inc(sem.panel_free, 1)

            act.dma_start(b.mrow[:, :, 0:D // 2], mem[0, :, 0:D // 2].rearrange("(t p) n -> p t n", p=P)
                          ).then_inc(sem.mem_half, 16)
            act.dma_start(b.mrow[:, :, D // 2:D], mem[0, :, D // 2:D].rearrange("(t p) n -> p t n", p=P)
                          ).then_inc(sem.mem_in, 16)
            act.dma_start(b.z[:, :, :], x[0].rearrange("(t p) n -> p t n", p=P)).then_inc(sem.x_in, 16)
            for i, v in enumerate((ln1_g, ln1_b, ln2_g, ln2_b)):
                act.dma_start(b.vrow[32 * i:32 * i + 32, 0, :], v.rearrange("l (k p) -> (l k) p", p=P)).then_inc(sem.vec_in, 16)
            for i, v in enumerate((mla_q_norm, mla_kv_norm)):
                act.dma_start(b.vrow[4 * i:4 * i + 4, 1, :], v.rearrange("l (k p) -> (l k) p", p=P)).then_inc(sem.vec_in, 16)
            act.dma_start(b.vrow[8:9, 1, :], gdn_o_norm).then_inc(sem.vec_in, 16)
            act.dma_start(b.vrow[9:9 + CB, 1, :], gdn_conv[0, TAPS - 1].rearrange("(k p) -> k p", p=P)).then_inc(sem.vec_in, 16)
            act.dma_start(b.vrow[0:3 * CB, 2, :],
                          gdn_conv[0, 0:TAPS - 1].rearrange("j (k p) -> (j k) p", p=P)).then_inc(sem.vec_in, 16)
            act.dma_start(b.alog[:, :], gdn_a_log.to_broadcast((P, NH))).then_inc(sem.gate_in, 16)
            act.dma_start(b.dtb[:, :], gdn_dt_bias.to_broadcast((P, NH))).then_inc(sem.gate_in, 16)
            act.dma_start(b.pos[:, :], positions_[0].rearrange("(t p) -> p t", p=P)).then_inc(sem.pos_in, 16)
            for k in range(8):
                if k % 2 == 0:
                    feed(1)
                split_turn(TURN_AT["mem0"] + k, b.hh, 2 * k)
            for k in range(PANEL):
                feed(1)
                split_turn(TURN_AT["x"] + k, b.xh, 2 * k)
            take_t("memk0", 0, b.km, 0, 1.0)
            act.wait_ge(sem.trig_set, 1)
            nc.scalar.activation(b.trig[:, :, :, :].rearrange("p a t c -> p (a t c)"),
                                 b.arg[:, :, :, :].rearrange("p a t c -> p (a t c)"), ACT.Sin).then_inc(sem.trig_out, 1)
            feed(PANEL)
            panel_end("memv0")
            for t in range(TT):
                last = nc.scalar.activation(b.vm[:, t, :], banks("memv0")[:, t, :], ACT.Copy)
            last.then_inc(sem.panel_free, 1)
            for name, dst in (("cq", b.cqrow), ("ckv", b.ckvrow)):
                feed(PANEL)
                panel_end(name)
                for t in range(TT):
                    last = nc.scalar.activation(dst[:, t, :], banks(name)[:, t, :], ACT.Copy)
                last.then_inc(sem.panel_free, 1)
            for k in range(2):
                split_turn(TURN_AT["cq"] + k, b.ch, 2 * k)
            feed(1)
            panel_end("kr")
            for t in range(TT):
                last = nc.scalar.activation(b.krow[:, t, :], banks("kr")[:, t, 0:ROPE], ACT.Copy)
            last.then_inc(sem.panel_free, 1)
            feed(PANEL)
            take_t("qm0", 0, b.qm, 0, scale_mem)
            for k in range(2):
                split_turn(TURN_AT["ckv"] + k, b.ch, 4 + 2 * k)
            act.wait_ge(sem.rot_t, 1)
            nc.scalar.activation(b.krt[:, :], pt_ps[:, 0:S], ACT.Copy).then_inc(sem.rot_out, 1)
            for i in range(2):
                feed(2)
                panel_end("qrope", i)
                for t in range(TT):
                    last = nc.scalar.activation(b.qrrow[:, t, 6 * i:6 * i + 6, :].rearrange("p h c -> p (h c)"),
                                                banks("qrope", i)[:, t, 0:6 * ROPE], ACT.Copy, scale=scale_mla)
                last.then_inc(sem.panel_free, 1)
            for i in range(3):
                feed(2)
                take_t("qnope", i, b.qn, 4 * i, scale_mla)
            for i in range(3):
                feed(2)
                take_t("knope", i, b.kn, 4 * i, 1.0)
            for i in range(3):
                feed(2)
                panel_end("v", i)
                for t in range(TT):
                    last = nc.scalar.activation(b.vrows[:, t, i * CN:(i + 1) * CN], banks("v", i)[:, t, :], ACT.Copy)
                last.then_inc(sem.panel_free, 1)
            for g in range(3):
                act.wait_ge(sem.rot_t, g + 2)
                nc.scalar.activation(b.qrt[:, 2 * g:2 * g + 2, :].rearrange("p k s -> p (k s)"), pt_ps[:, :],
                                     ACT.Copy).then_inc(sem.rot_out, 1)

            def exps(n):
                act.wait_ge(sem.bias_set, n + 1)
                if n >= 2:
                    act.wait_ge(sem.pt_done, n - 1)
                for t in range(TT):
                    last = nc.scalar.activation(b.prob[:, n % 2, t, :], turn_ps[n % 2][:, t * S:(t + 1) * S], ACT.Exp,
                                                bias=b.mx[:, n % 2, t:t + 1], accum_out=b.sums[:, n % 2, t:t + 1])
                last.then_inc(sem.exp_done, 1)

            def probs_out(n):
                act.wait_ge(sem.pt_done, n + 1)
                if n >= 2:
                    act.wait_ge(sem.o_done, n - 1)
                width = 2 * S if n >= NH else 2 * S - P
                nc.scalar.activation(b.probt[:, n % 2, 0:width], pt_ps[:, 0:width], ACT.Copy).then_inc(sem.pt_out, 1)

            def head_hi(n):
                act.wait_ge(sem.o_done, n + 1)
                nc.scalar.activation(b.hh[:, n if n < KT else n - NM, :], o_ps[:, 0:S], ACT.Copy).then_inc(sem.o_hi, 1)

            def attention(n0, n):
                for i in range(n0, n0 + n + 3):
                    if n0 <= i - 2 < n0 + n:
                        probs_out(i - 2)
                    if i < n0 + n:
                        exps(i)
                    if i - 3 >= n0:
                        head_hi(i - 3)

            attention(0, NH + NM)
            feed(UP * PANEL)

            def norm_block(k, j):
                act.wait_ge(sem.ln_rs, k + 1)
                for t in range(TT):
                    c = slice(j * CN, (j + 1) * CN)
                    nc.scalar.activation(b.z[:, t, c], b.z[:, t, c], ACT.Identity, bias=b.nmr[:, t:t + 1],
                                         scale=b.rs[:, t:t + 1]).then_inc(sem.ln_n, 1)

            def norm(k, name):
                norm_block(k, 0)
                for j in range(1, 4):
                    norm_block(k, j)
                    for i in (2 * j - 2, 2 * j - 1):
                        split_turn(TURN_AT[name] + i, b.xh, 2 * i)
                for i in (6, 7):
                    split_turn(TURN_AT[name] + i, b.xh, 2 * i)

            def mlp_group(l, name, g, last_group=False):
                c0, off = CHUNK_AT[name], g * GCH
                for u in range(2 * UP):
                    splits = PANEL - NSPLIT if last_group and u == 2 * UP - 1 else PANEL
                    for j in range(splits if u >= UP else PANEL - 1):
                        split(c0 + NSPLIT + u * PANEL + j, off)
                    if u >= UP:
                        continue
                    panel_end(name, u, off)
                    m = UP * GROUPS * l + u
                    if u >= 2:
                        act.wait_ge(sem.hid_lo, g * UP + (m - 1))
                    for j in range(2):
                        last = nc.scalar.activation(b.relu[:, u % 2, j * CN:(j + 1) * CN], banks(name, u)[:, j, :],
                                                    ACT.Relu)
                    last.then_inc(sem.panel_free, 1)
                    split(c0 + NSPLIT + u * PANEL + PANEL - 1, off)
                    act.wait_ge(sem.sq_done, g * UP + (m + 1))
                    nc.scalar.activation(b.hh[:, 4 * u:4 * u + 4, :].rearrange("p k s -> p (k s)"),
                                         b.relu[:, u % 2, :], ACT.Copy).then_inc(sem.hid_hi, 1)

            def mlp(l, name, last):
                with act.Fori(0, GROUPS - last) as g:
                    mlp_group(l, name, g)
                if last:
                    mlp_group(l, name, GROUPS - 1, True)

            norm(0, "ln1_0")
            mlp(0, "mlp0", LAST == 0)

            fed[0] = CHUNK_AT["memk1"] + NSPLIT
            act.wait_ge(sem.chunk_used, CHUNK_AT["memk1"])
            for k in range(8):
                split_turn(TURN_AT["mem1"] + k, b.hh, 2 * k)
                if k in (3, 5, 7):
                    feed(1)
            for j in range(4):
                norm_block(1, j)
                feed(1)
            feed(1)
            take_t("memk1", 0, b.km, 0, 1.0)
            for k in range(8):
                if k % 2 == 0:
                    feed(1)
                split_turn(TURN_AT["ln2_0"] + k, b.xh, 2 * k)
            feed(PANEL // 2)
            panel_end("memv1")
            for t in range(TT):
                last = nc.scalar.activation(b.vm[:, t, :], banks("memv1")[:, t, :], ACT.Copy)
            last.then_inc(sem.panel_free, 1)
            feed(1)
            panel_end("ab")
            for t in range(TT):
                last = nc.scalar.activation(b.arow[:, t, :], banks("ab")[:, t, 0:2 * NH], ACT.Copy)
            last.then_inc(sem.panel_free, 1)
            act.wait_ge(sem.gate_in, 32)
            nc.scalar.activation(b.alog[:, :], b.alog[:, :], ACT.Exp)
            act.wait_ge(sem.g_raw, 1)
            nc.scalar.activation(b.gt[:, :, :, :], b.gt[:, :, :, :], ACT.Exp).then_inc(sem.e_raw, 1)
            act.wait_ge(sem.g_raw, 2)
            nc.scalar.activation(b.gt[:, 0, :, :], b.gt[:, 0, :, :], ACT.Ln).then_inc(sem.l_raw, 1)
            act.wait_ge(sem.gcum_set, 1)
            nc.scalar.activation(b.eg[:, :, :], b.gcum[:, :, :], ACT.Exp)
            nc.scalar.activation(b.ek[:, :, :], b.ek[:, :, :], ACT.Exp)
            nc.scalar.activation(b.el[:, :, :], b.el[:, :, :], ACT.Exp).then_inc(sem.eg_set, 1)

            def taps(i):
                return lambda blk: vcol(1, 9 + blk) if i == TAPS - 1 else vcol(2, i * CB + blk)

            def conv(g, i):
                m = 3 * g + i
                name = "qkv"[i] + str(g)
                panel_end(name)
                if m:
                    act.wait_ge(sem.cv_t, m)
                for h in range(GH):
                    last = nc.scalar.activation(b.cv[:, h, :], banks(name)[:, h // 2, h % 2 * S:(h % 2 + 1) * S],
                                                ACT.Copy, scale=taps(TAPS - 1)(i * NH + g * GH + h))
                last.then_inc(sem.conv0, 1)
                act.wait_ge(sem.conv1, m + 1)
                nc.scalar.activation(b.th[:, :, :], b.cv[:, :, :], ACT.Tanh).then_inc(sem.tanh1, 1)

            def rows_out(g, i):
                m = 3 * g + i
                act.wait_ge(sem.cv_t, m + 1)
                dst = (b.qr, b.kr, b.vr)[i]
                for t in range(TT):
                    last = nc.scalar.activation(dst[:, t, :, :].rearrange("p h c -> p (h c)"),
                                                banks("qkv"[i] + str(g))[:, t, :], ACT.Copy)
                last.then_inc(sem.panel_free, 1)

            def z_rows(g):
                panel_end(f"z{g}")
                act.wait_ge(sem.cv_set, 3 * g + 3)
                zr = b.zr[:, :, :, :].rearrange("p t h c -> p t (h c)")
                for t in range(TT):
                    last = nc.scalar.activation(zr[:, t, :], banks(f"z{g}")[:, t, :], ACT.Copy, scale=0.5)
                last.then_inc(sem.panel_free, 1)
                act.wait_ge(sem.panel_free, PANEL_AT[f"z{g}"] + 1)
                nc.scalar.activation(b.th[:, :, :].rearrange("p h s -> p (h s)"),
                                     b.zr[:, :, :, :].rearrange("p t h c -> p (t h c)"), ACT.Tanh).then_inc(sem.z_tanh, 1)

            def bank_out(dst, t, ps, then, scale=1.0):
                nc.scalar.activation(dst[:, t].rearrange("p h c -> p (h c)"), ps[t][:, :], ACT.Copy,
                                     scale=scale).then_inc(then, 1)

            side_ps = [pt_ps, o_ps]

            def gdn(g):
                n0 = g * TT
                feed(4)
                rows_out(g, 2)
                for t in range(TT):
                    act.wait_ge(sem.p_kt, n0 + t + 1)
                    bank_out(b.kt, t, turn_ps, sem.a_kt)
                for t in range(TT):
                    act.wait_ge(sem.p_kbt, n0 + t + 1)
                    bank_out(b.kbt, t, side_ps, sem.a_kbt)
                for t in range(TT):
                    act.wait_ge(sem.p_qt, n0 + t + 1)
                    bank_out(b.qt, t, turn_ps, sem.a_qt)
                for t in range(TT):
                    act.wait_ge(sem.d_diff, n0 + t + 1)
                    nc.scalar.activation(b.dt[:, t], b.dt[:, t], ACT.Exp).then_inc(sem.a_dec, 1)
                for t in range(TT):
                    act.wait_ge(sem.p_qdt, n0 + t + 1)
                    bank_out(b.qdt, t, turn_ps, sem.a_qdt)
                feed(3)
                for l in range(LEVELS):
                    for t in range(TT):
                        m = (g * LEVELS + l) * TT + t
                        act.wait_ge(sem.p_y, m + 1)
                        if l > 1:
                            act.wait_ge(sem.p_zt, (g * (LEVELS - 1) + l - 2) * TT + t + 1)
                        bank_out(b.ys, t, turn_ps, sem.a_y)
                    if l:
                        feed(1)
                for t in range(TT):
                    act.wait_ge(sem.p_w, n0 + t + 1)
                    bank_out(b.wt, t, turn_ps, sem.a_w, scale=-1.0)
                z_rows(g)
                for j in range(NC):
                    if j:
                        feed(1)
                    r = slice(CHUNK * (j % 2), CHUNK * (j % 2 + 1))
                    act.wait_ge(sem.p_o, g * NC + j + 1)
                    nc.scalar.activation(b.orow[r, j // 2].rearrange("p h c -> p (h c)"), side_ps[j // 2][r, :],
                                         ACT.Copy).then_inc(sem.a_o, 1)
                feed(1)
                for k in range(2):
                    split_turn(TURN_AT[f"gdn{g}"] + k, b.hh, g * GH + 2 * k)

            feed(PANEL)
            act.wait_ge(sem.z_ready, 3)
            for g in range(HG):
                early = 3 if g else 0
                feed(early)
                conv(g, 0)
                feed(PANEL - 1 - early)
                rows_out(g, 0)
                feed(1)
                conv(g, 1)
                feed(PANEL // 2 + 1)
                rows_out(g, 1)
                feed(PANEL // 2 - 1)
                conv(g, 2)
                gdn(g)
            take_t("qm1", 0, b.qm, 0, scale_mem)
            attention(NH + NM, NM)
            feed(UP * PANEL)
            norm(2, "ln1_1")
            mlp(1, "mlp1", True)
            for j in range(4):
                norm_block(3, j)

        @block.vector
        def _(dve):
            steps = [0]

            def link(ins):
                steps[0] += 1
                ins.then_inc(sem.dve_step, 1)
                dve.wait_ge(sem.dve_step, steps[0])

            def split(c, off=0):
                dve.wait_ge(sem.hi_ready, off + (c + 1))
                nc.vector.tensor_tensor(b.wlo[:, c % NSPLIT], b.raw[:, c % NRAW], b.whi[:, c % NSPLIT].bitcast(F32),
                                        ALU.subtract).then_inc(sem.lo_ready, 1)

            fed = [0]

            def feed(k):
                for _ in range(k):
                    if fed[0] < CHUNKS:
                        split(fed[0])
                        fed[0] += 1

            def turn_out(g, kt, gain=None, bias=None):
                dve.wait_ge(sem.turned, g + 1)
                if g >= 2:
                    dve.wait_ge(sem.turn_lo, g - 1)
                if gain is None:
                    nc.vector.tensor_copy(b.xf[:, g % 2, :], turn_ps[g % 2][:, :]).then_inc(sem.turn_f, 1)
                    return
                for i in range(2):
                    c = slice(i * S, (i + 1) * S)
                    if bias is None:
                        last = nc.vector.tensor_scalar(b.xf[:, g % 2, c], turn_ps[g % 2][:, c], gain(kt + i), None,
                                                       ALU.mult)
                    else:
                        last = nc.vector.tensor_scalar(b.xf[:, g % 2, c], turn_ps[g % 2][:, c], gain(kt + i),
                                                       bias(kt + i), ALU.mult, ALU.add)
                last.then_inc(sem.turn_f, 1)

            for k in range(8):
                if k % 2 == 0:
                    feed(1)
                turn_out(TURN_AT["mem0"] + k, 2 * k)
            for k in range(PANEL):
                feed(1)
                turn_out(TURN_AT["x"] + k, 2 * k)
            dve.wait_ge(sem.vec_t, 1)
            nc.vector.tensor_copy(b.vcol[:, 0, :], pt_ps[:, 0:P])
            nc.vector.tensor_copy(b.vcol[:, 1, 0:9], pt_ps[:, P:P + 9])
            nc.vector.tensor_scalar(b.vcol[:, 1, 9:9 + CB], pt_ps[:, P + 9:P + 9 + CB], 0.5, None, ALU.mult)
            nc.vector.tensor_scalar(b.vcol[:, 2, 0:3 * CB], pt_ps[:, 2 * P:2 * P + 3 * CB], 0.5, None,
                                    ALU.mult).then_inc(sem.vcol_set, 1)

            dve.wait_ge(sem.pos_in, 16)
            dve.wait_ge(sem.const_set, 2)
            link(nc.vector.tensor_copy(b.posf[:, :], b.pos[:, :]))
            for t in range(TT):
                last = nc.vector.tensor_scalar(b.ang[:, t, :], b.invf[:, :], b.posf[:, t:t + 1], None, ALU.mult)
            link(last)
            magic = 1.5 * 2.0 ** 23
            two_pi = 2 * np.pi
            c1 = 6.28125
            c2 = float(np.float32(np.round((two_pi - c1) * 2.0 ** 21) / 2.0 ** 21))
            c3 = float(np.float32(two_pi - c1 - c2))
            ang = b.ang[:, :, :].rearrange("p t c -> p (t c)")
            for i, shift in ((0, 0.0), (1, 0.25)):
                k = b.turns[:, i].rearrange("p t c -> p (t c)")
                a = b.arg[:, i].rearrange("p t c -> p (t c)")
                link(nc.vector.tensor_scalar(k, ang, float(1 / two_pi), shift, ALU.mult, ALU.add))
                link(nc.vector.tensor_scalar(k, k, magic, None, ALU.add))
                link(nc.vector.tensor_scalar(k, k, magic, None, ALU.subtract))
                link(nc.vector.scalar_tensor_tensor(out=a, in0=k, scalar=-c1, in1=ang, op0=ALU.mult, op1=ALU.add))
                link(nc.vector.scalar_tensor_tensor(out=a, in0=k, scalar=-c2, in1=a, op0=ALU.mult, op1=ALU.add))
                link(nc.vector.scalar_tensor_tensor(out=a, in0=k, scalar=-c3, in1=a, op0=ALU.mult, op1=ALU.add))
                if i == 1:
                    link(nc.vector.tensor_scalar(a, a, float(np.pi / 2), None, ALU.add))
                last = nc.vector.tensor_scalar(a, a, 3.1415925, -3.1415925, ALU.min, ALU.max)
                if i == 0:
                    link(last)
            last.then_inc(sem.trig_set, 1)
            feed(PANEL)

            def row_norm(i, name, row):
                dve.wait_ge(sem.panel_free, PANEL_AT[name] + 1)
                link(nc.vector.tensor_tensor(b.csq[:, :, :], row[:, :, :], row[:, :, :], ALU.mult))
                nc.vector.tensor_reduce(b.css[:, i, :], b.csq[:, :, :], AX.X, ALU.add).then_inc(sem.c_sum, 1)
                dve.wait_ge(sem.c_rs, i + 1)
                for t in range(TT):
                    last = nc.vector.tensor_scalar(row[:, t, :], row[:, t, :], b.crs[:, i, t:t + 1], None, ALU.mult)
                last.then_inc(sem.c_norm, 1)

            feed(PANEL)
            row_norm(0, "cq", b.cqrow)
            feed(PANEL)
            for k in range(2):
                turn_out(TURN_AT["cq"] + k, 2 * k, gain=lambda kt: vcol(1, kt))
            row_norm(1, "ckv", b.ckvrow)
            feed(1)
            feed(PANEL)
            for k in range(2):
                turn_out(TURN_AT["ckv"] + k, 2 * k, gain=lambda kt: vcol(1, 4 + kt))
            feed(2 * (2 + 3 + 3 + 3))

            def maxima(n):
                dve.wait_ge(sem.scored, n + 1)
                if n >= 2:
                    dve.wait_ge(sem.exp_done, n - 1)
                nc.vector.tensor_reduce(b.mx[:, n % 2, :], turn_ps[n % 2][:, :].rearrange("p (t s) -> p t s", t=TT), AX.X,
                                        ALU.max, negate=True).then_inc(sem.bias_set, 1)

            def divide(n):
                dve.wait_ge(sem.exp_done, n + 1)
                link(nc.vector.reciprocal(b.rinv[:, n % 2, :], b.sums[:, n % 2, :]))
                for t in range(TT):
                    last = nc.vector.tensor_scalar(b.prob[:, n % 2, t, :], b.prob[:, n % 2, t, :],
                                                   b.rinv[:, n % 2, t:t + 1], None, ALU.mult)
                last.then_inc(sem.norm_done, 1)

            def head_lo(n):
                dve.wait_ge(sem.o_hi, n + 1)
                kt = n if n < KT else n - NM
                nc.vector.tensor_tensor(b.hl[:, kt, :], o_ps[:, 0:S], b.hh[:, kt, :].bitcast(F32),
                                        ALU.subtract).then_inc(sem.o_lo, 1)

            def attention(n0, n):
                for i in range(n0, n0 + n + 3):
                    if i < n0 + n:
                        maxima(i)
                    if n0 <= i - 1 < n0 + n:
                        divide(i - 1)
                    if i - 3 >= n0:
                        head_lo(i - 3)

            def add_rows(name, u, g=0):
                chunks = {n: c for n, _, c in STAGES}[name]
                dve.wait_ge(sem.chunk_used, g * GCH + (CHUNK_AT[name] + (u + 1) * chunks))
                c = slice(u % UP * CN, (u % UP + 1) * CN)
                for t in range(TT):
                    last = nc.vector.tensor_tensor(b.z[:, t, c], panel_ps[(PANEL_AT[name] + u) % 2][:, t, :], b.z[:, t, c],
                                                   ALU.add)
                last.then_inc(sem.panel_free, 1)
                dve.wait_ge(sem.panel_free, g * 2 * UP + (PANEL_AT[name] + u + 1))
                for t in range(TT):
                    nc.vector.bn_stats(b.stats[:, t, u % UP, :], b.z[:, t, c]).then_inc(sem.stats_in, 1)

            def stage_sums(panels):
                dve.wait_ge(sem.stats_in, TT * panels)
                for t in range(TT):
                    last = nc.vector.bn_aggr(b.mv[:, t, :], b.stats[:, t, :, :].rearrange("p a c -> p (a c)"))
                last.then_inc(sem.ln_mv, 1)

            attention(0, NH + NM)
            dve.wait_ge(sem.z_ready, 1)
            for u in range(UP):
                feed(PANEL - 1)
                add_rows("out0", u)
                if u == UP - 1:
                    stage_sums(UP)
                feed(1)

            def norm_out(name, l, which, splits=False):
                for i in range(8):
                    if splits and i % 2 == 0:
                        feed(1)
                    turn_out(TURN_AT[name] + i, 2 * i, gain=lambda kt: vcol(0, norm_cols("g" + which, l) + kt),
                             bias=lambda kt: vcol(0, norm_cols("b" + which, l) + kt))

            def mlp_group(l, name, g, last_group=False):
                c0, off = CHUNK_AT[name], g * GCH
                for u in range(2 * UP):
                    splits = PANEL - NSPLIT if last_group and u == 2 * UP - 1 else PANEL
                    for j in range(min(splits, PANEL - 1)):
                        split(c0 + NSPLIT + u * PANEL + j, off)
                    m = UP * GROUPS * l + u
                    if u < UP:
                        dve.wait_ge(sem.panel_free, g * 2 * UP + (PANEL_AT[name] + u + 1))
                        nc.vector.tensor_tensor(b.relu[:, u % 2, :], b.relu[:, u % 2, :], b.relu[:, u % 2, :],
                                                ALU.mult).then_inc(sem.sq_done, 1)
                    else:
                        if u == UP:
                            dve.wait_ge(sem.z_ready, 2 * l + 2)
                        add_rows(name, u, g)
                    if splits == PANEL:
                        split(c0 + NSPLIT + u * PANEL + PANEL - 1, off)

            def mlp(l, name, last):
                with dve.Fori(0, GROUPS - last) as g:
                    mlp_group(l, name, g)
                if last:
                    mlp_group(l, name, GROUPS - 1, True)

            norm_out("ln1_0", 0, "1")
            mlp(0, "mlp0", LAST == 0)

            fed[0] = CHUNK_AT["memk1"] + NSPLIT
            for k in range(8):
                turn_out(TURN_AT["mem1"] + k, 2 * k)
                if k == 1:
                    stage_sums(UP + UP * GROUPS)
                if k in (3, 5, 7):
                    feed(1)
            feed(5)
            norm_out("ln2_0", 0, "2", True)
            feed(PANEL // 2)
            feed(1)
            dve.wait_ge(sem.panel_free, PANEL_AT["ab"] + 1)
            dve.wait_ge(sem.gate_in, 32)
            a_rows, b_rows = b.arow[:, :, 0:NH], b.arow[:, :, NH:2 * NH]
            g0, g1 = b.gt[:, 0], b.gt[:, 1]
            link(nc.vector.tensor_tensor(a_rows, a_rows, b.dtb[:, :].unsqueeze(1).to_broadcast((P, TT, NH)), ALU.add))
            link(nc.vector.tensor_scalar(g0, a_rows, -1.0, None, ALU.mult))
            link(nc.vector.tensor_tensor(g0, g0, a_rows, ALU.min))
            nc.vector.tensor_scalar(g1, b_rows, -1.0, None, ALU.mult).then_inc(sem.g_raw, 1)
            dve.wait_ge(sem.e_raw, 1)
            link(nc.vector.tensor_scalar(b.gt[:, :, :, :], b.gt[:, :, :, :], 1.0, None, ALU.add))
            nc.vector.reciprocal(b.beta[:, :, :], g1).then_inc(sem.g_raw, 1)
            dve.wait_ge(sem.l_raw, 1)
            link(nc.vector.scalar_tensor_tensor(out=g0, in0=a_rows, scalar=0.0, in1=g0, op0=ALU.max, op1=ALU.add))
            link(nc.vector.tensor_tensor(g0, g0, b.alog[:, :].unsqueeze(1).to_broadcast((P, TT, NH)), ALU.mult))
            nc.vector.tensor_scalar(b.glog[:, :, :], g0, -1.0, None, ALU.mult).then_inc(sem.gates_set, 1)
            dve.wait_ge(sem.p_gc, 1)
            gcum = b.gcum[:, :, :].rearrange("p t h -> p (t h)")
            link(nc.vector.tensor_copy(gcum, turn_ps[0][:, 0:TT * NH]))
            nc.vector.tensor_tensor(b.ek[:, :, :].rearrange("p t h -> p (t h)"), turn_ps[0][:, 32:32 + TT * NH], gcum,
                                    ALU.subtract)
            nc.vector.tensor_copy(b.el[:, :, :].rearrange("p j h -> p (j h)"),
                                  turn_ps[1][:, 0:NC * NH]).then_inc(sem.gcum_set, 1)

            def conv(g, i):
                m = 3 * g + i
                p = PANEL_AT["qkv"[i] + str(g)]
                dve.wait_ge(sem.conv0, m + 1)
                for j in range(TAPS - 1):
                    shift = TAPS - 1 - j
                    for h in range(GH):
                        blk = i * NH + g * GH + h
                        ps = panel_ps[p % 2][:, h // 2, h % 2 * S:(h % 2 + 1) * S]
                        last = nc.vector.scalar_tensor_tensor(out=b.cv[:, h, shift:S], in0=ps[:, 0:S - shift],
                                                              scalar=vcol(2, j * CB + blk), in1=b.cv[:, h, shift:S],
                                                              op0=ALU.mult, op1=ALU.add)
                    if j < TAPS - 2:
                        link(last)
                last.then_inc(sem.conv1, 1)
                dve.wait_ge(sem.tanh1, m + 1)
                nc.vector.scalar_tensor_tensor(out=b.cv[:, :, :].rearrange("p h s -> p (h s)"),
                                               in0=b.th[:, :, :].rearrange("p h s -> p (h s)"), scalar=1.0,
                                               in1=b.cv[:, :, :].rearrange("p h s -> p (h s)"), op0=ALU.add,
                                               op1=ALU.mult).then_inc(sem.cv_set, 1)

            def flat(x_):
                return x_[:, :, :, :].rearrange("p t h c -> p (t h c)")

            def heads(x_):
                return x_[:, :, :, :].rearrange("p t h c -> p (t h) c")

            def per_head(x_, g):
                return x_[:, :, g * GH:(g + 1) * GH].unsqueeze(3).to_broadcast((P, TT, GH, P))

            def factor(i):
                return b.ss[:, i, :].rearrange("p (t h) -> p t h", t=TT).unsqueeze(3).to_broadcast((P, TT, GH, P))

            side_ps = [pt_ps, o_ps]

            def times(out_, x_, y_):
                return nc.vector.tensor_tensor(out_, x_, y_, ALU.mult)

            def row_sums(g, i):
                dve.wait_ge(sem.panel_free, PANEL_AT["qk"[i] + str(g)] + 1)
                rows = (b.qr, b.kr)[i]
                link(times(flat(b.dt), flat(rows), flat(rows)))
                link(nc.vector.tensor_reduce(b.ss[:, i, :], heads(b.dt), AX.X, ALU.add))

            def unit_rows(g):
                row_sums(g, 1)
                nc.vector.engine_nop().then_inc(sem.g_ss, 1)
                feed(1)
                dve.wait_ge(sem.g_rs, g + 1)
                link(times(b.kr[:, :, :, :], b.kr[:, :, :, :], factor(1)))
                times(b.qr[:, :, :, :], b.qr[:, :, :, :], factor(0)).then_inc(sem.kn_set, 1)

            def gdn(g):
                n0 = g * TT
                times(b.kb[:, :, :, :], b.kr[:, :, :, :], per_head(b.beta, g)).then_inc(sem.kb_set, 1)
                feed(4)
                dve.wait_ge(sem.panel_free, PANEL_AT[f"v{g}"] + 1)
                times(b.vr[:, :, :, :], b.vr[:, :, :, :], per_head(b.beta, g))
                for t in range(TT):
                    dve.wait_ge(sem.p_qt, n0 + t + 1)
                times(b.qr[:, :, :, :], b.qr[:, :, :, :], per_head(b.eg, g)).then_inc(sem.qd_set, 1)
                for t in range(TT):
                    dve.wait_ge(sem.p_gb, n0 + t + 1)
                    nc.vector.tensor_tensor(b.dt[:, t], side_ps[t][:, :].rearrange("p (h c) -> p h c", h=GH),
                                            b.gcum[:, t, g * GH:(g + 1) * GH].unsqueeze(2).to_broadcast((P, GH, P)),
                                            ALU.subtract).then_inc(sem.d_diff, 1)
                times(b.kb[:, :, :, :], b.kb[:, :, :, :], per_head(b.eg, g))
                times(b.kr[:, :, :, :], b.kr[:, :, :, :], per_head(b.ek, g)).then_inc(sem.kd_set, 1)
                feed(1)
                for t in range(TT):
                    dve.wait_ge(sem.p_l, n0 + t + 1)
                    dve.wait_ge(sem.a_dec, n0 + t + 1)
                    nc.vector.scalar_tensor_tensor(out=b.nt[:, t].rearrange("p h c -> p (h c)"), in0=side_ps[t][:, :],
                                                   scalar=-1.0, in1=b.dt[:, t].rearrange("p h c -> p (h c)"),
                                                   op0=ALU.mult, op1=ALU.mult).then_inc(sem.d_nt, 1)
                for t in range(TT):
                    dve.wait_ge(sem.p_aq, n0 + t + 1)
                    dve.wait_ge(sem.d_nt, n0 + t + 1)
                    times(b.aq[:, t].rearrange("p h c -> p (h c)"), turn_ps[t][:, :],
                          b.dt[:, t].rearrange("p h c -> p (h c)")).then_inc(sem.d_aq, 1)
                feed(2)
                eye = b.ident[:, :].unsqueeze(1).to_broadcast((P, GH, P))
                for l in range(LEVELS):
                    for t in range(TT):
                        m = (g * LEVELS + l) * TT + t
                        if l == 0:
                            dve.wait_ge(sem.bm_set, m + 1)
                            nc.vector.tensor_tensor(b.xt[:, t], b.bm[:, t], eye, ALU.add).then_inc(sem.d_xt, 1)
                            dve.wait_ge(sem.a_y, m + 1)
                            nc.vector.tensor_tensor(b.xi[:, t], b.ys[:, t], eye, ALU.add).then_inc(sem.d_x, 1)
                            continue
                        if l < LEVELS - 1:
                            dve.wait_ge(sem.p_z, (g * (LEVELS - 2) + l - 1) * TT + t + 1)
                            x_ = b.xi[:, t].rearrange("p h c -> p (h c)")
                            nc.vector.tensor_tensor(x_, turn_ps[t][:, :], x_, ALU.add).then_inc(sem.d_x, 1)
                        dve.wait_ge(sem.p_zt, (g * (LEVELS - 1) + l - 1) * TT + t + 1)
                        x_ = b.xt[:, t].rearrange("p h c -> p (h c)")
                        nc.vector.tensor_tensor(x_, side_ps[t][:, :], x_, ALU.add).then_inc(sem.d_xt, 1)
                    if l:
                        feed(1)
                for t in range(TT):
                    dve.wait_ge(sem.p_u, n0 + t + 1)
                    nc.vector.tensor_copy(b.uu[:, t].rearrange("p h c -> p (h c)"), side_ps[t][:, :]).then_inc(sem.d_u, 1)
                for j in range(NC):
                    t = j // 2
                    r = slice(CHUNK * (j % 2), CHUNK * (j % 2 + 1))
                    vn = b.vn[r, 0].rearrange("p h c -> p (h c)")
                    uu = b.uu[r, t].rearrange("p h c -> p (h c)")
                    if j == 0:
                        dve.wait_ge(sem.d_u, n0 + 1)
                        nc.vector.tensor_copy(vn, uu).then_inc(sem.d_vn, 1)
                    else:
                        dve.wait_ge(sem.p_vn, g * (NC - 1) + j)
                        if j == 2:
                            dve.wait_ge(sem.d_u, n0 + 2)
                        nc.vector.tensor_tensor(vn, turn_ps[0][r, :], uu, ALU.add).then_inc(sem.d_vn, 1)
                    if j == NC - 1:
                        break
                    if j == 2:
                        dve.wait_ge(sem.z_tanh, g + 1)
                        nc.vector.scalar_tensor_tensor(out=flat(b.zr), in0=b.th[:, :, :].rearrange("p h s -> p (h s)"),
                                                       scalar=1.0, in1=flat(b.zr), op0=ALU.add, op1=ALU.mult)
                    dve.wait_ge(sem.p_ds, g * (NC - 1) + j + 1)
                    nxt = b.st[:, (j + 1) % 2].rearrange("p h c -> p (h c)")
                    if j == 0:
                        nc.vector.tensor_copy(nxt, turn_ps[1][:, :]).then_inc(sem.d_s, 1)
                    else:
                        dve.wait_ge(sem.pool_s, g * (NC - 2) + j)
                        nc.vector.tensor_tensor(nxt, turn_ps[1][:, :], b.st[:, 2].rearrange("p h c -> p (h c)"),
                                                ALU.add).then_inc(sem.d_s, 1)
                        feed(1)
                feed(1)
                dve.wait_ge(sem.a_o, (g + 1) * NC)
                link(times(flat(b.nt), flat(b.orow), flat(b.orow)))
                nc.vector.tensor_reduce(b.ss[:, 2, :], heads(b.nt), AX.X, ALU.add).then_inc(sem.o_ss, 1)
                feed(1)
                dve.wait_ge(sem.o_rs, g + 1)
                link(times(b.orow[:, :, :, :], b.orow[:, :, :, :], factor(2)))
                times(flat(b.orow), flat(b.orow), flat(b.zr)).then_inc(sem.or_set, 1)
                for k in range(2):
                    turn_out(TURN_AT[f"gdn{g}"] + k, 0, gain=lambda kt: vcol(1, 8))

            feed(PANEL)
            dve.wait_ge(sem.z_ready, 3)
            dve.wait_ge(sem.eg_set, 1)
            for g in range(HG):
                early = 3 if g else 0
                feed(early)
                conv(g, 0)
                feed(PANEL - early)
                conv(g, 1)
                feed(3)
                row_sums(g, 0)
                feed(2)
                unit_rows(g)
                feed(2)
                conv(g, 2)
                gdn(g)
            attention(NH + NM, NM)
            for u in range(UP):
                feed(PANEL - 1)
                add_rows("out1", u)
                if u == UP - 1:
                    stage_sums(2 * UP + UP * GROUPS)
                feed(1)
            norm_out("ln1_1", 1, "1")
            mlp(1, "mlp1", True)
            stage_sums(2 * (UP + UP * GROUPS))

            def finish(k):
                dve.wait_ge(sem.gb_in, 32 * k)
                for j in range(4):
                    for t in range(TT):
                        c = slice(j * CN, (j + 1) * CN)
                        dve.wait_ge(sem.ln_n, 8 * (k - 1) + 2 * j + t + 1)
                        link(nc.vector.tensor_tensor(b.z[:, t, c], b.z[:, t, c], b.gb[:, 0, c], ALU.mult))
                        nc.vector.tensor_tensor(b.z[:, t, c], b.z[:, t, c], b.gb[:, 1, c], ALU.add).then_inc(sem.fin, 1)

            finish(4)

        @block.gpsimd
        def _(pool):
            steps = [0]

            def link(ins):
                steps[0] += 1
                ins.then_inc(sem.pool_step, 1)
                pool.wait_ge(sem.pool_step, steps[0])

            for m in (b.ident, b.identb):
                link(nc.gpsimd.memset(m[:, :], 0.0))
                link(nc.gpsimd.affine_select(out=m[:, :], in_=m[:, :], compare_op=ALU.not_equal, fill=1.0, base=0,
                                             pattern=[[-1, P]], channel_multiplier=1))
                if m is b.ident:
                    nc.gpsimd.engine_nop().then_inc(sem.const_set, 1)
            link(nc.gpsimd.memset(b.causal[:, :, :], 0.0))
            link(nc.gpsimd.affine_select(out=b.causal[:, :, :], in_=b.causal[:, :, :], compare_op=ALU.is_ge, fill=NEG,
                                         base=0, pattern=[[P, TT], [-1, S]], channel_multiplier=1))
            freq = 1.0 / (np.float32(ROPE_THETA) ** (np.arange(0, ROPE, 2, dtype=np.float32) / np.float32(ROPE)))
            for i in range(HR):
                nc.gpsimd.memset(b.invf[:, i:i + 1], float(np.float32(freq[i])))
            nc.gpsimd.memset(b.mhalf[:, :], -0.5).then_inc(sem.const_set, 1)

            def turn_lo(g, hi, lo, kt):
                pool.wait_ge(sem.turn_hi, g + 1)
                nc.gpsimd.tensor_tensor(lo[:, kt:kt + 2, :].rearrange("p k s -> p (k s)"), b.xf[:, g % 2, :],
                                        hi[:, kt:kt + 2, :].rearrange("p k s -> p (k s)").bitcast(F32),
                                        ALU.subtract).then_inc(sem.turn_lo, 1)

            def rsqrt(out_, in_, scale, eps, n):
                link(nc.gpsimd.tensor_scalar(out_, in_, scale, eps, ALU.mult, ALU.add))
                return nc.gpsimd.tensor_tensor(out_, out_, b.mhalf[:, 0:n], ALU.pow)

            for k in range(8):
                turn_lo(TURN_AT["mem0"] + k, b.hh, b.hl, 2 * k)
            for k in range(8):
                turn_lo(TURN_AT["x"] + k, b.xh, b.xl, 2 * k)

            def same(m, s):
                link(nc.gpsimd.memset(m, 1.0))
                v = m.rearrange("p (k c) -> p k c", c=s)
                for base, row, blk in ((0, 1, -s), (s - 1, -1, s)):
                    link(nc.gpsimd.affine_select(out=v, in_=v, compare_op=ALU.is_ge, fill=0.0, base=base,
                                                 pattern=[[blk, P // s], [0, s]], channel_multiplier=row))

            link(nc.gpsimd.memset(b.ones[:, :], 1.0))
            link(nc.gpsimd.tensor_copy(b.tri[:, :], b.ident[:, :]))
            for l in range(LEVELS):
                same(b.blk[:, :], 2 << l)
                m = b.level[:, l, :]
                link(nc.gpsimd.tensor_tensor(m, b.blk[:, :], b.tri[:, :], ALU.subtract))
                link(nc.gpsimd.affine_select(out=m, in_=m, compare_op=ALU.is_ge, fill=0.0, base=0, pattern=[[1, P]],
                                             channel_multiplier=-1))
                link(nc.gpsimd.tensor_copy(b.tri[:, :], b.blk[:, :]))
            link(nc.gpsimd.affine_select(out=b.tri[:, :], in_=b.tri[:, :], compare_op=ALU.is_ge, fill=0.0, base=0,
                                         pattern=[[1, P]], channel_multiplier=-1))
            nc.gpsimd.tensor_scalar(b.negtri[:, :], b.tri[:, :], -NEG, NEG, ALU.mult, ALU.add).then_inc(sem.masks_set, 1)
            nc.gpsimd.tensor_scalar(b.z[:, :, :].rearrange("p t n -> p (t n)"), b.z[:, :, :].rearrange("p t n -> p (t n)"),
                                    ALPHA, None, ALU.mult).then_inc(sem.z_ready, 1)

            def row_rs(i):
                pool.wait_ge(sem.c_sum, i + 1)
                rsqrt(b.crs[:, i, :], b.css[:, i, :], 1.0 / LORA, RMS_EPS, TT).then_inc(sem.c_rs, 1)

            def rotate(x1, x2, t, n, o1, o2):
                sin, cos = (b.trig[:, i, t, :].unsqueeze(1).to_broadcast((P, n, HR)) for i in range(2))
                tmp = [b.rtmp[:, i, 0:n * HR].rearrange("p (n c) -> p n c", c=HR) for i in range(4)]
                nc.gpsimd.tensor_tensor(tmp[0], x1, cos, ALU.mult)
                nc.gpsimd.tensor_tensor(tmp[1], x2, sin, ALU.mult)
                nc.gpsimd.tensor_tensor(tmp[2], x2, cos, ALU.mult)
                link(nc.gpsimd.tensor_tensor(tmp[3], x1, sin, ALU.mult))
                nc.gpsimd.tensor_tensor(o1, tmp[0], tmp[1], ALU.subtract)
                return nc.gpsimd.tensor_tensor(o2, tmp[2], tmp[3], ALU.add)

            row_rs(0)
            for k in range(2):
                turn_lo(TURN_AT["cq"] + k, b.ch, b.cl, 2 * k)
            row_rs(1)
            pool.wait_ge(sem.trig_out, 1)
            pool.wait_ge(sem.panel_free, PANEL_AT["kr"] + 1)
            for t in range(TT):
                link(rotate(b.krow[:, t, 0:HR].unsqueeze(1), b.krow[:, t, HR:ROPE].unsqueeze(1), t, 1,
                            b.krot[:, t, 0:1, 0:HR], b.krot[:, t, 0:1, HR:ROPE]))
            nc.gpsimd.tensor_copy(b.krot[:, :, 1, :], b.krot[:, :, 0, :]).then_inc(sem.rot_done, 1)
            for k in range(2):
                turn_lo(TURN_AT["ckv"] + k, b.ch, b.cl, 4 + 2 * k)
            pool.wait_ge(sem.panel_free, PANEL_AT["qnope"])
            for t in range(TT):
                ins = rotate(b.qrrow[:, t, :, 0:HR], b.qrrow[:, t, :, HR:ROPE], t, NH, b.qrrow[:, t, :, 0:HR],
                             b.qrrow[:, t, :, HR:ROPE])
                ins.then_inc(sem.rot_done, 1)
                pool.wait_ge(sem.rot_done, 2 + t)

            def norm_factors(k):
                pool.wait_ge(sem.ln_mv, k + 1)
                link(rsqrt(b.rs[:, :], b.mv[:, :, 1], 1.0, LN_EPS, TT))
                link(nc.gpsimd.tensor_tensor(b.nmr[:, :], b.mv[:, :, 0], b.rs[:, :], ALU.mult))
                nc.gpsimd.tensor_scalar(b.nmr[:, :], b.nmr[:, :], -1.0, None, ALU.mult).then_inc(sem.ln_rs, 1)

            def norm(k, name):
                for i in range(8):
                    turn_lo(TURN_AT[name] + i, b.xh, b.xl, 2 * i)
                gb = b.gb[:, :, :].rearrange("p a n -> p (a n)")
                pool.wait_ge(sem.gb_in, 32 * (k + 1))
                link(nc.gpsimd.tensor_scalar(gb, gb, ALPHA, None, ALU.mult))
                for t in range(TT):
                    link(nc.gpsimd.tensor_tensor(b.z[:, t, :], b.z[:, t, :], b.gb[:, 0, :], ALU.mult))
                    last = nc.gpsimd.tensor_tensor(b.z[:, t, :], b.z[:, t, :], b.gb[:, 1, :], ALU.add)
                last.then_inc(sem.z_ready, 1)

            def mlp(l):
                with pool.Fori(0, GROUPS) as g:
                    for u in range(UP):
                        pool.wait_ge(sem.hid_hi, g * UP + (UP * GROUPS * l + u + 1))
                        nc.gpsimd.tensor_tensor(b.hl[:, 4 * u:4 * u + 4, :].rearrange("p k s -> p (k s)"),
                                                b.relu[:, u % 2, :],
                                                b.hh[:, 4 * u:4 * u + 4, :].rearrange("p k s -> p (k s)").bitcast(F32),
                                                ALU.subtract).then_inc(sem.hid_lo, 1)

            norm_factors(0)
            norm(0, "ln1_0")
            mlp(0)
            for k in range(8):
                turn_lo(TURN_AT["mem1"] + k, b.hh, b.hl, 2 * k)
                if k == 1:
                    norm_factors(1)
            norm(1, "ln2_0")

            def gdn(g):
                n0 = g * TT
                for t in range(TT):
                    if g:
                        pool.wait_ge(sem.or_set, g)
                    nc.gpsimd.tensor_tensor(b.tg[:, t], b.tri[:, :].unsqueeze(1).to_broadcast((P, GH, P)),
                                            b.glog[:, t, g * GH:(g + 1) * GH].unsqueeze(2).to_broadcast((P, GH, P)),
                                            ALU.mult).then_inc(sem.tg_set, 1)
                pool.wait_ge(sem.g_ss, g + 1)
                link(rsqrt(b.ss[:, 0:2, :].rearrange("p a h -> p (a h)"), b.ss[:, 0:2, :].rearrange("p a h -> p (a h)"),
                           1.0, 1e-6, 2 * TT * GH))
                nc.gpsimd.tensor_scalar(b.ss[:, 0, :], b.ss[:, 0, :], float(P) ** -0.5, None, ALU.mult).then_inc(sem.g_rs, 1)
                for l in range(LEVELS):
                    for t in range(TT):
                        pool.wait_ge(sem.d_nt, n0 + t + 1)
                        if l:
                            pool.wait_ge(sem.p_y, (g * LEVELS + l - 1) * TT + t + 1)
                            if l == 1:
                                pool.wait_ge(sem.d_xt, g * LEVELS * TT + t + 1)
                        else:
                            pool.wait_ge(sem.p_qdt, n0 + t + 1)
                        nc.gpsimd.tensor_tensor(b.bm[:, t], b.nt[:, t],
                                                b.level[:, l, :].unsqueeze(1).to_broadcast((P, GH, P)),
                                                ALU.mult).then_inc(sem.bm_set, 1)
                for j in range(1, NC - 1):
                    pool.wait_ge(sem.d_s, g * (NC - 1) + j)
                    nc.gpsimd.tensor_tensor(b.st[:, 2], b.st[:, j % 2],
                                            b.el[:, j, g * GH:(g + 1) * GH].unsqueeze(2).to_broadcast((P, GH, P)),
                                            ALU.mult).then_inc(sem.pool_s, 1)
                pool.wait_ge(sem.o_ss, g + 1)
                rsqrt(b.ss[:, 2, :], b.ss[:, 2, :], 1.0 / P, RMS_EPS, TT * GH).then_inc(sem.o_rs, 1)
                for k in range(2):
                    turn_lo(TURN_AT[f"gdn{g}"] + k, b.hh, b.hl, g * GH + 2 * k)

            pool.wait_ge(sem.gates_set, 1)
            pool.wait_ge(sem.eg_set, 1)
            for g in range(HG):
                gdn(g)
            norm_factors(2)
            norm(2, "ln1_1")
            mlp(1)
            norm_factors(3)


_INS = ["x", "mem", "positions", "mla_w_in", "mla_q_norm", "mla_w_uq", "mla_kv_norm", "mla_w_ukv", "gdn_w_in",
        "gdn_conv", "gdn_a_log", "gdn_dt_bias", "gdn_o_norm", "mem_w_kv", "w_out", "ln1_g", "ln1_b", "mlp_w1",
        "mlp_w2", "ln2_g", "ln2_b"]


def kernel(**inputs):
    import numpy as _np
    import concourse.bacc as _bacc
    from concourse import mybir as _mybir
    from concourse.bass_utils import run_bass_kernel_spmd as _run

    nc = _bacc.Bacc("TRN2", target_bir_lowering=False, num_devices=1)
    arrays, args = {}, []
    for name in _INS:
        a = _np.ascontiguousarray(inputs[name])
        arrays[f"in_{name}"] = a
        args.append(nc.dram_tensor(f"in_{name}", a.shape, _mybir.dt.from_np(a.dtype), kind="ExternalInput").ap())
    args.append(nc.dram_tensor("out", (1, S, D), _mybir.dt.float32, kind="ExternalOutput").ap())
    build(nc, *args)
    r = _run(nc, [arrays], core_ids=[0])
    return r.results[0]["out"]
```
